# Optimizing a Trainium2 kernel written in Bass

```python
import math
import jax, jax.numpy as jnp
from jax import lax
import numpy as np

D_MODEL = 1024
BATCH = 1
SEQ = 512
DEPTH = 2

ATTN_HEADS = 8
HEAD_DIM = 64
ATTN_WIDTH = ATTN_HEADS * HEAD_DIM
DILATED_PATTERNS = ((128, 1), (512, 4), (2048, 16))
REL_BUCKETS = 32
REL_MAX_DISTANCE = 1024
SSD_HEADS = 16
SSD_HEADDIM = 64
SSD_INNER = SSD_HEADS * SSD_HEADDIM
SSD_GROUPS = 2
SSD_STATE = 128
SSD_XBC = SSD_INNER + 2 * SSD_GROUPS * SSD_STATE
SSD_CONV = 7
SSD_CHUNK = 128
SC_WIDTH = 512
SC_CONV = 3
MIX_WIDTH = ATTN_WIDTH + SSD_INNER + SC_WIDTH
N_IN = 3 * ATTN_WIDTH + SSD_INNER + SSD_XBC + 2 * SSD_HEADS + 3 * SC_WIDTH
D_FF = 2816
FFN_CONV = 3
EPS = 1e-6
NEG_INF = -1e30

kernel_name = "hybrid_dilated_ssd_shortconv_encoder"

def rmsnorm(x, g):
    xf = x.astype(jnp.float32)
    y = xf * lax.rsqrt(jnp.mean(xf * xf, axis=-1, keepdims=True) + EPS)
    return (y * g.astype(jnp.float32)).astype(x.dtype)

def dwconv(x, w, b):
    k = w.shape[0]
    pad = k // 2
    y = lax.conv_general_dilated(x, w[:, None, :].astype(x.dtype), window_strides=(1,),
                                 padding=[(pad, pad)], dimension_numbers=('NWC', 'WIO', 'NWC'),
                                 feature_group_count=x.shape[-1])
    return y + b.astype(x.dtype)

def t5_bucket(rel):
    nb = REL_BUCKETS // 2
    max_exact = nb // 2
    ret = jnp.where(rel > 0, nb, 0)
    n = jnp.abs(rel)
    nf = jnp.maximum(n, 1).astype(jnp.float32)
    large = max_exact + (jnp.log(nf / max_exact) / math.log(REL_MAX_DISTANCE / max_exact)
                         * (nb - max_exact)).astype(jnp.int32)
    large = jnp.minimum(large, nb - 1)
    return ret + jnp.where(n < max_exact, n, large)

def dilated_attention(q, k, v, rel_table, window, dil):
    b, s, h, e = q.shape
    r = (window // 2) // dil
    blk = r
    L = s // dil
    nb = -(-L // blk)
    lp = nb * blk

    def to_sub(t, lo, hi):
        t = t.reshape(b, L, dil, h, e).transpose(0, 2, 1, 3, 4)
        return jnp.pad(t, ((0, 0), (0, 0), (lo, hi), (0, 0), (0, 0)))

    qb = to_sub(q, 0, lp - L).reshape(b, dil, nb, blk, h, e)

    def band(t):
        tb = to_sub(t, blk, lp - L + blk).reshape(b, dil, nb + 2, blk, h, e)
        return jnp.concatenate([tb[:, :, :-2], tb[:, :, 1:-1], tb[:, :, 2:]], axis=3)

    kb, vb = band(k), band(v)
    qi = jnp.arange(blk)[:, None]
    ki = jnp.arange(3 * blk)[None, :] - blk
    rel = ki - qi
    bias = rel_table[t5_bucket(rel * dil)].astype(jnp.float32).transpose(2, 0, 1)
    kpos = jnp.arange(nb)[:, None, None] * blk + ki[None]
    valid = (jnp.abs(rel) <= r)[None] & (kpos >= 0) & (kpos < L)

    scores = jnp.einsum('brnqhe,brnkhe->brhnqk', qb, kb) + bias[:, None]
    scores = jnp.where(valid, scores, NEG_INF)
    m = jnp.max(scores, axis=-1, keepdims=True)
    p = jnp.exp(scores - m)
    den = jnp.sum(p, axis=-1)
    o = jnp.einsum('brhnqk,brnkhe->brnqhe', p, vb) / jnp.moveaxis(den, 2, -1)[..., None]
    lse = jnp.moveaxis(m[..., 0] + jnp.log(den), 2, -1)

    def from_sub(t):
        t = t.reshape((b, dil, lp) + t.shape[4:])[:, :, :L]
        return jnp.swapaxes(t, 1, 2).reshape((b, s) + t.shape[3:])

    return from_sub(o), from_sub(lse)

def attention_mixer(q, k, v, q_g, k_g, rel_table):
    b, s, _ = q.shape
    heads = lambda t: t.reshape(b, s, ATTN_HEADS, HEAD_DIM)
    qf = rmsnorm(heads(q), q_g).astype(jnp.float32) * (HEAD_DIM ** -0.5)
    kf = rmsnorm(heads(k), k_g).astype(jnp.float32)
    vf = heads(v).astype(jnp.float32)
    res = [dilated_attention(qf, kf, vf, rel_table, w, d) for (w, d) in DILATED_PATTERNS]
    outs = jnp.stack([o for (o, _) in res])
    lses = jnp.stack([l for (_, l) in res])
    wts = jax.nn.softmax(lses, axis=0)
    o = jnp.sum(wts[..., None] * outs, axis=0)
    return o.reshape(b, s, ATTN_WIDTH).astype(q.dtype)

def ssd_chunked(xs, dt, a, bm, cm):
    b, s, h, p = xs.shape
    g, n = bm.shape[2], bm.shape[3]
    e = h // g
    t = SSD_CHUNK
    c = s // t
    X = (xs * dt[..., None]).reshape(b, c, t, g, e, p)
    a_cs = jnp.cumsum((dt * a).reshape(b, c, t, g, e), axis=2)
    Bc = bm.reshape(b, c, t, g, n)
    Cc = cm.reshape(b, c, t, g, n)
    lower = jnp.tril(jnp.ones((t, t), dtype=bool))[None, None, :, :, None, None]
    seg = a_cs[:, :, :, None] - a_cs[:, :, None, :]
    decay = jnp.exp(jnp.where(lower, seg, -jnp.inf))
    cb = jnp.einsum('bclgn,bcsgn->bclsg', Cc, Bc)
    y_diag = jnp.einsum('bclsge,bcsgep->bclgep', cb[..., None] * decay, X)
    x_to_end = X * jnp.exp(a_cs[:, :, -1:] - a_cs)[..., None]
    states = jnp.einsum('bcsgn,bcsgep->bcgepn', Bc, x_to_end)
    chunk_decay = jnp.exp(a_cs[:, :, -1])

    def carry_state(state, inp):
        st, dec = inp
        return state * dec[..., None, None] + st, state

    _, s_in = lax.scan(carry_state, jnp.zeros_like(states[:, 0]),
                       (jnp.moveaxis(states, 1, 0), jnp.moveaxis(chunk_decay, 1, 0)))
    s_in = jnp.moveaxis(s_in, 0, 1)
    y_off = jnp.einsum('bclgn,bcgepn->bclgep', Cc, s_in) * jnp.exp(a_cs)[..., None]
    return (y_diag + y_off).reshape(b, s, h, p)

def ssd_mixer(z, xbc, dt_raw, conv_w, conv_b, dt_bias, a_log, d_skip, norm_g):
    b, s, _ = z.shape
    f32 = jnp.float32
    xbc = jax.nn.silu(dwconv(xbc, conv_w, conv_b)).astype(f32)
    xs, bm, cm = jnp.split(xbc, [SSD_INNER, SSD_INNER + SSD_GROUPS * SSD_STATE], axis=-1)
    xs = xs.reshape(b, s, SSD_HEADS, SSD_HEADDIM)
    bm = bm.reshape(b, s, SSD_GROUPS, SSD_STATE)
    cm = cm.reshape(b, s, SSD_GROUPS, SSD_STATE)
    dt = jax.nn.softplus(dt_raw.astype(f32).reshape(b, s, 2, SSD_HEADS) + dt_bias.astype(f32))
    a = -jnp.exp(a_log.astype(f32))
    flip = lambda t: jnp.flip(t, axis=1)
    y_fwd = ssd_chunked(xs, dt[:, :, 0], a[0], bm, cm)
    y_bwd = flip(ssd_chunked(flip(xs), flip(dt[:, :, 1]), a[1], flip(bm), flip(cm)))
    y = y_fwd + y_bwd + d_skip.astype(f32)[:, None] * xs
    gsz = SSD_INNER // SSD_GROUPS
    y = y.reshape(b, s, SSD_GROUPS, gsz) * jax.nn.silu(z.astype(f32)).reshape(b, s, SSD_GROUPS, gsz)
    y = y * lax.rsqrt(jnp.mean(y * y, axis=-1, keepdims=True) + EPS)
    y = y.reshape(b, s, SSD_INNER) * norm_g.astype(f32)
    return y.astype(z.dtype)

def short_conv_mixer(gate_b, gate_c, xin, conv_w, conv_b):
    return gate_b * dwconv(gate_c * xin, conv_w, conv_b)

def conv_ffn(h, w_up, conv_w, conv_b, w_down):
    u = dwconv(h @ w_up, conv_w, conv_b)
    gate, val = jnp.split(u, 2, axis=-1)
    return (jax.nn.silu(gate) * val) @ w_down

def setup_inputs(seed: int = 0) -> dict:
    key = jax.random.key(seed)
    ks = jax.random.split(key, 24)
    nrm = lambda k, shape: jax.random.normal(k, shape, jnp.float32)
    dt0 = jnp.exp(jax.random.uniform(ks[8], (DEPTH, 2, SSD_HEADS), jnp.float32,
                                     math.log(1e-3), math.log(1e-1)))
    return {
        "x": nrm(ks[0], (BATCH, SEQ, D_MODEL)),
        "rel_table": 0.5 * nrm(ks[1], (REL_BUCKETS, ATTN_HEADS)),
        "norm1_g": 1.0 + 0.1 * nrm(ks[2], (DEPTH, D_MODEL)),
        "w_in": nrm(ks[3], (DEPTH, D_MODEL, N_IN)) * D_MODEL ** -0.5,
        "q_norm_g": 1.0 + 0.1 * nrm(ks[4], (DEPTH, HEAD_DIM)),
        "k_norm_g": 1.0 + 0.1 * nrm(ks[5], (DEPTH, HEAD_DIM)),
        "ssd_conv_w": nrm(ks[6], (DEPTH, SSD_CONV, SSD_XBC)) * SSD_CONV ** -0.5,
        "ssd_conv_b": 0.01 * nrm(ks[7], (DEPTH, SSD_XBC)),
        "ssd_dt_bias": dt0 + jnp.log(-jnp.expm1(-dt0)),
        "ssd_a_log": jnp.log(jax.random.uniform(ks[9], (DEPTH, 2, SSD_HEADS), jnp.float32, 1.0, 16.0)),
        "ssd_d": 1.0 + 0.1 * nrm(ks[10], (DEPTH, SSD_HEADS)),
        "ssd_norm_g": 1.0 + 0.1 * nrm(ks[11], (DEPTH, SSD_INNER)),
        "sc_conv_w": nrm(ks[12], (DEPTH, SC_CONV, SC_WIDTH)) * SC_CONV ** -0.5,
        "sc_conv_b": 0.01 * nrm(ks[13], (DEPTH, SC_WIDTH)),
        "w_out": nrm(ks[14], (DEPTH, MIX_WIDTH, D_MODEL)) * MIX_WIDTH ** -0.5,
        "norm2_g": 1.0 + 0.1 * nrm(ks[15], (DEPTH, D_MODEL)),
        "ffn_w_up": nrm(ks[16], (DEPTH, D_MODEL, 2 * D_FF)) * D_MODEL ** -0.5,
        "ffn_conv_w": nrm(ks[17], (DEPTH, FFN_CONV, 2 * D_FF)) * FFN_CONV ** -0.5,
        "ffn_conv_b": 0.01 * nrm(ks[18], (DEPTH, 2 * D_FF)),
        "ffn_w_down": nrm(ks[19], (DEPTH, D_FF, D_MODEL)) * D_FF ** -0.5,
    }

def reference(x, rel_table, norm1_g, w_in, q_norm_g, k_norm_g, ssd_conv_w, ssd_conv_b,
              ssd_dt_bias, ssd_a_log, ssd_d, ssd_norm_g, sc_conv_w, sc_conv_b, w_out,
              norm2_g, ffn_w_up, ffn_conv_w, ffn_conv_b, ffn_w_down):
    split_at = list(np.cumsum([ATTN_WIDTH, ATTN_WIDTH, ATTN_WIDTH, SSD_INNER, SSD_XBC,
                               2 * SSD_HEADS, SC_WIDTH, SC_WIDTH]))
    for i in range(DEPTH):
        h = rmsnorm(x, norm1_g[i])
        u = h @ w_in[i]
        q, k, v, z, xbc, dt_raw, sc_b, sc_c, sc_x = jnp.split(u, split_at, axis=-1)
        a_out = attention_mixer(q, k, v, q_norm_g[i], k_norm_g[i], rel_table)
        s_out = ssd_mixer(z, xbc, dt_raw, ssd_conv_w[i], ssd_conv_b[i], ssd_dt_bias[i],
                          ssd_a_log[i], ssd_d[i], ssd_norm_g[i])
        c_out = short_conv_mixer(sc_b, sc_c, sc_x, sc_conv_w[i], sc_conv_b[i])
        x = x + jnp.concatenate([a_out, s_out, c_out], axis=-1) @ w_out[i]
        x = x + conv_ffn(rmsnorm(x, norm2_g[i]), ffn_w_up[i], ffn_conv_w[i], ffn_conv_b[i], ffn_w_down[i])
    return x


_drawn_inputs = setup_inputs


def setup_inputs(seed=0):
    import zlib

    import numpy as np

    out = dict(_drawn_inputs(seed))
    spreads = {}
    factors = {'q_norm_g': 6.744,
     'k_norm_g': 5.996,
     'ssd_conv_b': 3.958,
     'sc_conv_b': 8.0,
     'ffn_conv_b': 6.478}
    for name, (base, spread) in spreads.items():
        noise = np.random.default_rng([zlib.crc32(name.encode()), seed]).standard_normal(out[name].shape)
        drawn = base * np.exp(spread * noise) if base else spread * noise
        out[name] = __import__('jax').numpy.asarray(drawn.astype(out[name].dtype))
    for name, factor in factors.items():
        out[name] = (out[name] * factor).astype(out[name].dtype)
    return out
```

```python
import math
from contextlib import ExitStack

import numpy as np

import concourse.bass as bass
from concourse import mybir

F32, F32R = mybir.dt.float32, mybir.dt.float32r
ACT, ALU = mybir.ActivationFunctionType, mybir.AluOpType
P = 128

D_MODEL, SEQ, DEPTH = 1024, 512, 2
HEADS, HEAD_DIM = 8, 64
PATTERNS = ((128, 1), (512, 4), (2048, 16))
BUCKETS, MAX_DISTANCE = 32, 1024
SSD_HEADS, SSD_GROUPS = 16, 2
SSD_TAPS, D_FF = 7, 2816
EPS, NEG = 1e-6, -1e30
ATTN_W, SSD_W, SC_W = 512, 1024, 512

KT = D_MODEL // P
QT = SEQ // P
CHUNK = KT * P
FF_T = D_FF // P
DOWN_C = -(-FF_T // KT)
DIR = 32
REL = 2 * SEQ
TOEP = 2 * SEQ - P

C_XBC, C_QK, C_V, C_Z, C_SC = 0, 12, 20, 24, 32
C_DT, C_OUT = 44, 46
C_UP = C_OUT + 2 * KT
C_DOWN = C_UP + 2 * FF_T
C_END = C_DOWN + DOWN_C * KT
N_IN = C_DT
N_XBC, N_QK, N_Z, N_SC = 0, 12, 20, 28
N_OUT = 40
N_UP = N_OUT
N_DOWN = N_UP + 2 * FF_T

_at = 0


def _cols(n):
    global _at
    _at += n
    return _at - n


PA_N1, PA_N2, PA_QG, PA_KG = _cols(KT), _cols(KT), _cols(1), _cols(1)
PA_CONV7, PA_D, PA_SNG = _cols(12 * 8), _cols(8), _cols(8)
PA_SC, PA_FF = _cols(4 * 4), _cols(2 * FF_T * 4)
PA_DTB, PA_ALOG = _cols(64), _cols(64)
PA_N = _at

CONSTS = ("ident", "ones", "le", "ge", "gt", "lt", "headones")
RMS_BASE = {"norm1": 0, "ssd0": 8, "ssd1": 12, "norm2": 16}
RMS_TILES = {"norm1": KT, "ssd0": 4, "ssd1": 4, "norm2": KT}


class Steps:

    def __init__(self, eng, sem):
        self.eng, self.sem, self.n, self.turn = eng, sem, 0, None

    def __call__(self, ins):
        ins.then_inc(self.sem, 1)
        self.n += 1
        self.eng.wait_ge(self.sem, self.value())

    def value(self):
        return self.n if self.turn is None else self.turn[0] * self.turn[1] + self.n

    def enter(self, turn, per_turn):
        self.turn, self.start = (turn, per_turn), self.n

    def leave(self, turns):
        per_turn = self.turn[1]
        assert self.n - self.start == per_turn, (self.n - self.start, per_turn)
        self.turn, self.n = None, self.start + turns * per_turn


def build_trunk(nc, a):
    ctx = ExitStack()

    def sb(name, shape, dt=F32):
        return ctx.enter_context(nc.sbuf_tensor(f"sb_{name}", shape, dt))

    def sem(name):
        return ctx.enter_context(nc.semaphore(name))

    def overlay(name, *groups):
        found, most = {}, 0
        for group in groups:
            size = 0
            with ExitStack() as st:
                for n, shape, dt in group:
                    found[n] = st.enter_context(nc.sbuf_tensor(f"sb_{n}", shape, dt))
                    size += 4 * math.prod(shape[1:])
            most = max(most, size)
        sb(name, [P, most // 4])
        return found

    X = sb("x_stream", [P, KT, SEQ])
    CON = sb("constants", [P, len(CONSTS), P])
    con = {n: CON[:, i, :] for i, n in enumerate(CONSTS)}
    IDR = sb("ident_r", [P, P], F32R)
    PAR = sb("params", [P, PA_N])
    EPSC = sb("eps_columns", [P, 2])
    W = sb("w_raw", [P, 2, CHUNK])
    WHI = sb("w_hi", [P, 2, CHUNK], F32R)
    WLO = sb("w_lo", [P, 2, CHUNK], F32R)
    T = sb("t_normed", [P, 2, SEQ])
    SQ = sb("squares", [P, 2, SEQ])
    RSTD = sb("rstd", [P, SEQ])
    DT = sb("dt", [P, QT, 64])
    DA = sb("dt_a", [P, QT, 64])
    SM = sb("small", [P, 4, QT * 64])
    EW = sb("decays", [P, QT, P])
    WS = sb("state_weights", [P, QT, 64])
    AS = sb("cumsum_columns", [P, QT, 64])
    NEGMAX = sb("neg_max", [P, 4])
    DEN = sb("softmax_sums", [P, 4])
    RDEN = sb("softmax_recips", [P, 4])

    o1 = overlay(
        "region_h",
        [("h_hi", [P, KT, SEQ], F32R), ("h_lo", [P, KT, SEQ], F32R)],
        [("probs_t", [P, 2, QT, SEQ], F32), ("bias_t", [P, 2, TOEP], F32)],
        [("x_tok", [P, QT, SSD_W], F32), ("b_tok", [P, QT, 256], F32), ("cs_hi", [P, SEQ], F32R),
         ("cs_lo", [P, SEQ], F32R), ("exp_cs", [P, 2, 2, SEQ], F32)],
    )
    HHI, HLO = o1["h_hi"], o1["h_lo"]
    PTS, BIAS = o1["probs_t"], o1["bias_t"]
    XT, BT, CSHI, CSLO, EA = (o1[n] for n in ("x_tok", "b_tok", "cs_hi", "cs_lo", "exp_cs"))
    o2 = overlay(
        "region_m",
        [("ff_hi", [P, FF_T, SEQ], F32R), ("ff_lo", [P, FF_T, SEQ], F32R), ("ff_gate", [P, 2, SEQ], F32),
         ("ff_val", [P, 2, SEQ], F32), ("ff_silu", [P, SEQ], F32), ("ff_prod", [P, SEQ], F32)],
        [("mh_ssd", [P, 8, SEQ], F32R), ("ml_ssd", [P, 8, SEQ], F32R), ("mh_at", [P, 4, SEQ], F32R),
         ("ml_at", [P, 4, SEQ], F32R), ("mh_sc", [P, 4, SEQ], F32R), ("ml_sc", [P, 4, SEQ], F32R)],
        [("z", [P, 8, SEQ], F32), ("xc", [P, 8, SEQ], F32), ("q", [P, 4, SEQ], F32), ("k", [P, 4, SEQ], F32),
         ("qk_sq", [P, 8, SEQ], F32), ("bc", [P, 4, SEQ], F32), ("v", [P, QT, ATTN_W], F32),
         ("conv_acc", [P, 2, SEQ], F32), ("sc_c", [P, SEQ], F32), ("sc_cx", [P, SEQ], F32),
         ("sc_acc", [P, SEQ], F32), ("sc_prod", [P, SEQ], F32)],
        [("pad_a", [P, 36, SEQ], F32), ("cb", [P, 2, SEQ], F32), ("s_in", [P, 2, 3, SEQ], F32),
         ("x_scaled", [P, 2, SEQ], F32), ("e", [P, 2, 2, SEQ], F32)],
        [("pad_b", [P, 40, SEQ], F32), ("scores", [P, 2, SEQ], F32), ("probs", [P, 2, SEQ], F32)],
        [("pad_c", [P, 42, SEQ], F32), ("onehot", [BUCKETS, REL], F32), ("log_count", [HEADS, REL], F32), ("table", [BUCKETS, HEADS], F32),
         ("bias_row", [HEADS, REL], F32)],
    )
    FHI, FLO, FG, FV, FS, FP = (o2[n] for n in ("ff_hi", "ff_lo", "ff_gate", "ff_val", "ff_silu", "ff_prod"))
    Z, XC, Q, K, QKSQ, BC, V = (o2[n] for n in ("z", "xc", "q", "k", "qk_sq", "bc", "v"))
    ACC7, SCC, CX, SCA, SCP = (o2[n] for n in ("conv_acc", "sc_c", "sc_cx", "sc_acc", "sc_prod"))
    CB, SIN, XS, E = (o2[n] for n in ("cb", "s_in", "x_scaled", "e"))
    S, PR = o2["scores"], o2["probs"]

    def mixed(part, k):
        where = "at" if k < 4 else "ssd" if k < 12 else "sc"
        return o2[f"m{part}_{where}"][:, k - (0 if k < 4 else 4 if k < 12 else 12), :]

    BANK = ctx.enter_context(nc.psum_tensor("banks", [P, 8, SEQ], F32))

    def bank(i):
        return BANK[:, i, :]

    scratch = nc.dram_tensor("bias_rows", [HEADS, P, REL], F32).ap()

    layer_go = sem("layer_go")
    x_stored = sem("x_stored")
    con_landed, x_landed, setup_landed = sem("con_landed"), sem("x_landed"), sem("setup_landed")
    idr_done, eps_done = sem("idr_done"), sem("eps_done")
    bias_mm, bias_row, bias_stored = sem("bias_mm"), sem("bias_row"), sem("bias_stored")
    first_cleared = layer_end = sem("layer_end")
    par_landed = sem("par_landed")
    w_landed = [sem("w_landed0"), sem("w_landed1")]
    w_hi, w_lo = sem("w_hi"), sem("w_lo")
    w_used = sem("w_used")
    evac = [sem("evac0"), sem("evac1")]
    dve_step = sem("dve_step")
    sq_done, ss_done, root_done = sem("sq_done"), sem("ss_done"), sem("root_done")
    t_done = sem("t_done")
    n_hi, n_lo = sem("n_hi"), sem("n_lo")
    x_added = sem("x_added")
    tap_first, silu_done = sem("tap_first"), sem("silu_done")
    qk_sq, qk_ss, qk_root, qk_norm = sem("qk_sq"), sem("qk_ss"), sem("qk_root"), sem("qk_norm")
    v_copied = sem("v_copied")
    cx_tap, sc_hi, sc_lo = sem("cx_tap"), sem("sc_hi_done"), sem("sc_lo_done")
    bias_landed = [sem("bias_landed0"), sem("bias_landed1")]
    at_qk, at_neg, at_exp, at_p = sem("at_qk"), sem("at_neg"), sem("at_exp"), sem("at_p")
    at_tr, at_ptc, at_pv, at_hi, at_lo = sem("at_tr"), sem("at_ptc"), sem("at_pv"), sem("at_hi"), sem("at_lo")
    dt_x, dt_e, dt_w, dt_ln, a_exp, da_done = (sem(n) for n in ("dt_x", "dt_e", "dt_w", "dt_ln", "a_exp", "da_done"))
    cs_mm, cs_row, cs_hi, cs_lo, cs_tr, cs_col = (sem(n) for n in ("cs_mm", "cs_row", "cs_hi_done", "cs_lo_done", "cs_tr", "cs_col"))
    dec_mm, dec_exp, ws_done = sem("dec_mm"), sem("dec_exp"), sem("ws_done")
    tok_tr, tok_copied = sem("tok_tr"), sem("tok_copied")
    cb_mm, cb_done, xs_done, st_mm, sin_done = (sem(n) for n in ("cb_mm", "cb_done", "xs_done", "st_mm", "sin_done"))
    ab_mm, seg_done, clamp_done, e_done, ea_done = (sem(n) for n in ("ab_mm", "seg_done", "clamp_done", "e_done", "ea_done"))
    g_done, gs_done, y_mm, yo_mm, y_comb = (sem(n) for n in ("g_done", "gs_done", "y_mm", "yo_mm", "y_comb"))
    ff_tap, ff_silu, ff_hi, ff_lo = (sem(n) for n in ("ff_tap", "ff_silu_done", "ff_hi_done", "ff_lo_done"))
    last_cleared = ff_lo

    def par(col, n=1):
        return PAR[:, col:col + n] if isinstance(col, int) else PAR[:, bass.ds(col, n)]

    def tile_of(tensor, t):
        if isinstance(t, int):
            return tensor[:, t, :]
        return tensor[:, bass.ds(t, 1), :].rearrange("p a s -> p (a s)")

    def column(d, h):
        return d * DIR + h

    def direction_chunk(j):
        d, i = j % 2, j // 2
        return d, (i if d == 0 else QT - 1 - i)

    def rms_hi(name, k):
        if name in ("norm1", "norm2"):
            return HHI[:, k, :]
        return o2["mh_ssd"][:, 4 * int(name[-1]) + k, :]

    def rms_bank(name):
        return bank(6 if name[0] == "n" else 0)

    block = ctx.enter_context(nc.Block())

    @block.sync
    def _(sp):
        sp.dma_start(CON[:, :, :], a["constants"]).then_inc(con_landed, 16)
        sp.dma_start(X[:, :, :], a["x_t"].rearrange("(k p) s -> p k s", p=P)).then_inc(x_landed, 16)
        sp.dma_start(o2["onehot"][:, :], a["onehot"]).then_inc(setup_landed, 16)
        sp.dma_start(o2["log_count"][:, :], a["log_count"]).then_inc(setup_landed, 16)
        sp.dma_start(o2["table"][:, :], a["rel_table"]).then_inc(setup_landed, 16)
        sp.wait_ge(bias_row, 2)
        sp.dma_start(scratch, o2["bias_row"][:, :].unsqueeze(1).to_broadcast([HEADS, P, REL])).then_inc(bias_stored, 16)

        def load(src, row, b, chunk, n=CHUNK, first=False):
            if not first:
                sp.wait_ge(w_lo, chunk - 1)
            sp.dma_start(W[:, b, 0:n], src[bass.ds(row, 1), :, 0:n].rearrange("a p n -> p (a n)"))\
                .then_inc(w_landed[b], 16)

        sp.sem_inc(layer_go, 1)
        with sp.Fori(0, DEPTH) as layer:
            sp.wait_ge(layer_go, layer + 1)
            sp.nop(nofuse=True)
            sp.dma_start(PAR[:, :], a["params"][bass.ds(layer, 1), :, :].rearrange("a p n -> p (a n)"))\
                .then_inc(par_landed, 16)
            for b in range(2):
                load(a["w_in"], layer * C_DT + b, b, b, first=True)
            with sp.Fori(0, C_DT // 2 - 1) as i:
                for b in range(2):
                    load(a["w_in"], layer * C_DT + (i * 2 + (2 + b)), b, i * 2 + (2 + b))
            for b in range(2):
                load(a["w_dt"], layer * 2 + b, b, C_DT + b, n=KT // 2 * 64)
            for b in range(2):
                load(a["w_out"], layer * (2 * KT) + b, b, C_OUT + b)
            sp.wait_ge(bias_stored, 16)
            for h in range(HEADS):
                if h < 2:
                    sp.wait_ge(w_used, C_OUT)
                else:
                    sp.wait_ge(at_neg, 4 * (h - 1))
                sp.dma_start(BIAS[:, h % 2, :], bass.AP(scratch.tensor, h * P * REL + P - 1, [[REL - 1, P], [1, TOEP]]))\
                    .then_inc(bias_landed[h % 2], 16)
            with sp.Fori(0, KT - 1) as i:
                for b in range(2):
                    load(a["w_out"], layer * (2 * KT) + (i * 2 + (2 + b)), b, i * 2 + (C_OUT + 2 + b))
            with sp.Fori(0, FF_T) as i:
                for b in range(2):
                    load(a["w_up"], layer * (2 * FF_T) + (i * 2 + b), b, i * 2 + (C_UP + b))
            with sp.Fori(0, KT // 2) as i:
                for j in range(2 * DOWN_C):
                    last = j % DOWN_C == DOWN_C - 1
                    load(a["w_down"], layer * (DOWN_C * KT) + (i * (2 * DOWN_C) + j), j % 2, i * (2 * DOWN_C) + (C_DOWN + j),
                         n=(FF_T - (DOWN_C - 1) * KT) * P if last else CHUNK)
            sp.wait_ge(layer_end, 4)
            sp.sem_clear(range(first_cleared.num, last_cleared.num + 1))
            sp.sem_inc(layer_go, 1)
        sp.dma_start(a["out_t"].rearrange("(k p) s -> p k s", p=P), X[:, :, :]).then_inc(x_stored, 16)
        sp.wait_ge(x_stored, 16)

    @block.gpsimd
    def _(pool):
        g = nc.gpsimd

        def w_low(b, done):
            pool.wait_ge(w_hi, done)
            g.tensor_tensor(WLO[:, b, :], W[:, b, :], WHI[:, b, :].bitcast(F32), ALU.subtract).then_inc(w_lo, 1)

        def low_next(first, count):
            with pool.Fori(0, count // 2) as i:
                for b in range(2):
                    w_low(b, i * 2 + (first + b + 3))

        def rms_low(name, dst):
            for k in range(RMS_TILES[name]):
                at = RMS_BASE[name] + k
                pool.wait_ge(n_hi, at + 1)
                g.tensor_tensor(dst(k), T[:, at % 2, :], rms_hi(name, k).bitcast(F32), ALU.subtract).then_inc(n_lo, 1)

        with pool.Fori(0, DEPTH) as layer:
            pool.wait_ge(layer_go, layer + 1)
            pool.nop(nofuse=True)
            pool.sem_inc(sc_lo, 1)
            pool.sem_inc(ff_lo, 1)
            w_low(0, 1)
            rms_low("norm1", lambda k: HLO[:, k, :])
            w_low(1, 2)
            low_next(0, C_SC)
            with pool.Fori(0, 2) as i:
                for j in range(6):
                    w_low(j % 2, i * 6 + (C_SC + j + 3))
                    if j % 3 == 2:
                        t = i * 2 + j // 3
                        pool.wait_ge(sc_hi, t + 2)
                        g.tensor_tensor(tile_of(o2["ml_sc"], t), SCP[:, :], tile_of(o2["mh_sc"], t).bitcast(F32),
                                        ALU.subtract).then_inc(sc_lo, 1)
            for b in range(2):
                w_low(b, C_DT + b + 3)

            pool.wait_ge(sc_lo, 5)
            for grp in range(SSD_GROUPS):
                for j in range(6):
                    d, c = direction_chunk(j)
                    n, col = grp * 6 + j, column(d, 8 * grp)
                    pool.wait_ge(ws_done, 1)
                    pool.wait_ge(tok_copied, 8)
                    if n >= 2:
                        pool.wait_ge(st_mm, n - 1)
                    g.tensor_tensor(XS[:, j % 2, :].rearrange("p (h e) -> p h e", e=64),
                                    XT[:, c, 512 * grp:512 * grp + 512].rearrange("p (h e) -> p h e", e=64),
                                    WS[:, c, col:col + 8].unsqueeze(2).to_broadcast([P, 8, 64]), ALU.mult)\
                        .then_inc(xs_done, 1)
                for hh in range(8 + 1):
                    h = 8 * grp + hh
                    if hh < 8:
                        for d in range(2):
                            pool.wait_ge(seg_done, 2 * h + d + 1)
                            g.tensor_scalar(E[:, d, h % 2, :], E[:, d, h % 2, :], 0.0, None, ALU.min).then_inc(clamp_done, 1)
                    if hh >= 1:
                        pool.wait_ge(g_done, h)
                        g.tensor_tensor(E[:, 0, (h - 1) % 2, :], E[:, 0, (h - 1) % 2, :], E[:, 1, (h - 1) % 2, :], ALU.add)\
                            .then_inc(gs_done, 1)
                rms_low(f"ssd{grp}", lambda k: o2["ml_ssd"][:, 4 * grp + k, :])
            low_next(C_OUT, 2 * KT)
            rms_low("norm2", lambda k: HLO[:, k, :])
            with pool.Fori(0, FF_T // 2) as i:
                for j in range(4):
                    w_low(j % 2, i * 4 + (C_UP + j + 3))
                    if j % 2 == 1:
                        t = i * 2 + j // 2
                        pool.wait_ge(ff_hi, t + 2)
                        g.tensor_tensor(tile_of(FLO, t), FP[:, :], tile_of(FHI, t).bitcast(F32), ALU.subtract)\
                            .then_inc(ff_lo, 1)
            low_next(C_DOWN, DOWN_C * KT - 2)
            pool.drain().then_inc(layer_end, 1)

    @block.scalar
    def _(act):
        sc = nc.scalar

        def w_high(b, landed):
            act.wait_ge(w_landed[b], landed)
            sc.activation(WHI[:, b, :], W[:, b, :], ACT.Copy).then_inc(w_hi, 1)

        def high_next(c, i=0, step=0):
            act.wait_ge(w_used, i * step + (c + 1))
            w_high(c % 2, i * (8 * step) + 16 * (c // 2 + 2))

        def rms(name, src, mean_scale, ready=None):
            base, n = RMS_BASE[name], RMS_TILES[name]
            for k in range(n):
                if ready is not None:
                    ready(k)
                if base + k >= 2:
                    act.wait_ge(ss_done, base + k - 1)
                sc.activation(SQ[:, k % 2, :], src(k), ACT.Square).then_inc(sq_done, 1)
            act.wait_ge(ss_done, base + n)
            sc.activation(RSTD[:, :], rms_bank(name), ACT.Sqrt, bias=EPSC[:, 0:1], scale=mean_scale).then_inc(root_done, 1)
            for k in range(n):
                act.wait_ge(t_done, base + k + 1)
                sc.activation(rms_hi(name, k), T[:, k % 2, :], ACT.Copy).then_inc(n_hi, 1)

        act.wait_ge(con_landed, 16)
        sc.activation(IDR[:, :], con["ident"], ACT.Copy).then_inc(idr_done, 1)
        act.wait_ge(eps_done, 2)
        act.wait_ge(x_landed, 16)
        with act.Fori(0, DEPTH) as layer:
            act.wait_ge(layer_go, layer + 1)
            act.nop(nofuse=True)
            act.wait_ge(par_landed, 16)
            w_high(0, 16)
            rms("norm1", lambda k: X[:, k, :], 1.0 / D_MODEL)
            w_high(1, 16)

            def centre_tap(b, tile, acc_read=None):
                if acc_read is not None:
                    act.wait_ge(silu_done, acc_read)
                col = tile * 8 + PA_CONV7
                sc.activation(ACC7[:, b, :], bank(b), ACT.Identity, bias=par(col + 7), scale=par(col + 3)).then_inc(tap_first, 1)

            def silu(b, dst, done):
                act.wait_ge(evac[b], done)
                sc.activation(dst, ACC7[:, b, :], ACT.Silu).then_inc(silu_done, 1)

            high_next(0)
            centre_tap(0, 0)
            high_next(1)
            centre_tap(1, 1)
            silu(0, XC[:, 0, :], 1)
            with act.Fori(0, 3) as i:
                for b in range(2):
                    high_next(2 + b, i, 2)
                    centre_tap(b, i * 2 + (2 + b), i * 2 + (1 + b))
                    silu(1 - b, tile_of(XC, i * 2 + (1 + b)), i + (1 + b))
            for n in range(8, 12):
                high_next(n)
                centre_tap(n % 2, n, n - 1)
                silu((n - 1) % 2, XC[:, 7, :] if n == 8 else BC[:, n - 9, :], (n - 1) // 2 + 1)
            silu(1, BC[:, 3, :], 6)

            for dst, c in ((Q, C_QK), (K, C_QK + 4)):
                with act.Fori(0, 2) as i:
                    for b in range(2):
                        high_next(c + b, i, 2)
                        sc.activation(tile_of(dst, i * 2 + b), bank(b), ACT.Copy).then_inc(evac[b], 1)
            for j in range(4):
                high_next(C_V + j)
            for c in range(QT):
                sc.activation(V[:, c, :], bank(2 + c), ACT.Copy).then_inc(v_copied, 1)
            for n in range(8):
                act.wait_ge(qk_ss, n + 1)
                sc.activation(QKSQ[:, n, :], bank(6 + n % 2), ACT.Sqrt, bias=EPSC[:, 1 - n // 4:2 - n // 4],
                              scale=1.0 if n < 4 else 1.0 / HEAD_DIM).then_inc(qk_root, 1)
            with act.Fori(0, 4) as i:
                for b in range(2):
                    high_next(C_Z + b, i, 2)
                    sc.activation(tile_of(Z, i * 2 + b), bank(b), ACT.Silu).then_inc(evac[b], 1)
            act.wait_ge(bias_stored, 16)
            with act.Fori(0, 2) as i:
                for j in range(6):
                    t = i * 2 + j // 3
                    high_next(C_SC + j, i, 6)
                    if j % 3 == 0:
                        act.wait_ge(evac[j % 2], i * 3 + (N_SC + j - 2) // 2 + 1)
                        sc.activation(SCC[:, :], bank(j % 2), ACT.Copy).then_inc(evac[j % 2], 1)
                    if j % 3 == 1:
                        act.wait_ge(evac[j % 2], i * 3 + ((N_SC + j) // 2 + 1))
                        act.wait_ge(sc_hi, t + 1)
                        sc.activation(SCA[:, :], CX[:, :], ACT.Identity, bias=par(t * 4 + (PA_SC + 3)),
                                      scale=par(t * 4 + (PA_SC + 1))).then_inc(cx_tap, 1)
            for b in range(2):
                high_next(C_DT + b)

            act.wait_ge(dt_x, 1)
            sc.activation(SM[:, 1, :], SM[:, 1, :], ACT.Exp).then_inc(dt_e, 1)
            sc.activation(par(PA_ALOG, 64), par(PA_ALOG, 64), ACT.Exp).then_inc(a_exp, 1)
            act.wait_ge(dt_w, 1)
            sc.activation(SM[:, 3, :], SM[:, 2, :], ACT.Ln).then_inc(dt_ln, 1)

            def at_evac(u):
                h, qt = u // 4, u % 4
                act.wait_ge(at_tr, u + 1)
                if h >= 2:
                    act.wait_ge(at_pv, h - 1)
                sc.activation(PTS[:, h % 2, :, qt * P:qt * P + P], bank(4 + u % 2).rearrange("p (j i) -> p j i", i=P),
                              ACT.Copy).then_inc(at_ptc, 1)

            def at_out(t):
                act.wait_ge(at_pv, 2 * t + 2)
                sc.activation(o2["mh_at"][:, t, :], bank(6 + t % 2), ACT.Copy).then_inc(at_hi, 1)

            for u in range(4 * HEADS):
                act.wait_ge(at_neg, u + 1)
                if u >= 2:
                    act.wait_ge(at_tr, u - 1)
                sc.activation(PR[:, u % 2, :], S[:, u % 2, :], ACT.Exp, bias=NEGMAX[:, u % 4:u % 4 + 1], scale=-1.0,
                              accum_out=DEN[:, u % 4:u % 4 + 1]).then_inc(at_exp, 1)
                if u >= 1:
                    at_evac(u - 1)
                if u % 8 == 3 and u > 8:
                    at_out(u // 8 - 1)
            at_evac(4 * HEADS - 1)
            at_out(HEADS // 2 - 1)

            act.wait_ge(cs_mm, 1)
            sc.activation(T[0:64, 0, :], BANK[0:64, 2, :], ACT.Copy).then_inc(cs_row, 1)
            sc.activation(CSHI[0:64, :], BANK[0:64, 2, :], ACT.Copy).then_inc(cs_hi, 1)
            act.wait_ge(dec_mm, 1)
            sc.activation(EW[:, :, :], bank(4).rearrange("p (c n) -> p c n", n=P), ACT.Exp).then_inc(dec_exp, 1)
            act.wait_ge(cs_tr, 1)
            sc.activation(AS[:, :, :], BANK[:, 3, 0:256].rearrange("p (c n) -> p c n", n=64), ACT.Copy).then_inc(cs_col, 1)
            for n in range(10):
                act.wait_ge(tok_tr, n + 1)
                if n < 8:
                    dst, src = XT[:, n // 2, (n % 2) * 512:(n % 2) * 512 + 512], bank(5 + n % 2)
                else:
                    dst, src = BT[:, 2 * (n - 8):2 * (n - 8) + 2, :], bank(5 + n % 2).rearrange("p (c n) -> p c n", n=256)
                sc.activation(dst, src, ACT.Copy).then_inc(tok_copied, 1)
            for grp in range(SSD_GROUPS):
                for hh in range(8):
                    h = 8 * grp + hh
                    half = 64 * (h % 2)
                    for d in range(2):
                        if h >= 4:
                            act.wait_ge(y_comb, h // 2 - 1)
                        act.wait_ge(seg_done, 2 * h + d + 1)
                        sc.activation(EA[half:half + 64, d, (h // 2) % 2, :], BANK[half:half + 64, 2 + 2 * (h % 2) + d, :],
                                      ACT.Exp).then_inc(ea_done, 1)
                        act.wait_ge(clamp_done, 2 * h + d + 1)
                        sc.activation(E[:, d, h % 2, :], E[:, d, h % 2, :], ACT.Exp).then_inc(e_done, 1)
                rms(f"ssd{grp}", lambda k: Z[:, 4 * grp + k, :], 1.0 / 512, lambda k: act.wait_ge(y_comb, 4 * grp + k + 1))

            with act.Fori(0, KT) as i:
                for b in range(2):
                    high_next(C_OUT + b, i, 2)
            rms("norm2", lambda k: X[:, k, :], 1.0 / D_MODEL, lambda k: act.wait_ge(x_added, k + 1))

            with act.Fori(0, FF_T // 2) as i:
                for j in range(4):
                    pb, t, col = j // 2, i * 2 + j // 2, i * 16 + (PA_FF + 4 * j)
                    high_next(C_UP + j, i, 4)
                    sc.activation((FG, FV)[j % 2][:, pb, :], bank(j % 2), ACT.Identity, bias=par(col + 3), scale=par(col + 1))\
                        .then_inc(ff_tap, 1)
                    if j % 2 == 1:
                        act.wait_ge(evac[0], t + (N_UP // 2 + 1))
                        act.wait_ge(ff_hi, t + 1)
                        sc.activation(FS[:, :], FG[:, pb, :], ACT.Silu).then_inc(ff_silu, 1)
            with act.Fori(0, (DOWN_C * KT - 2) // 2) as i:
                for b in range(2):
                    high_next(C_DOWN + b, i, 2)
            act.drain().then_inc(layer_end, 1)

    @block.vector
    def _(dve):
        v = nc.vector
        v.memset(EPSC[:, 0:1], EPS).then_inc(eps_done, 1)
        v.memset(EPSC[:, 1:2], EPS * HEAD_DIM).then_inc(eps_done, 1)
        dve.wait_ge(setup_landed, 48)
        for r in range(2):
            dve.wait_ge(bias_mm, r + 1)
            v.tensor_tensor(o2["bias_row"][:, 512 * r:512 * r + 512], BANK[0:HEADS, r, :],
                            o2["log_count"][:, 512 * r:512 * r + 512], ALU.add).then_inc(bias_row, 1)
        dve.wait_ge(x_landed, 16)
        dve.wait_ge(con_landed, 16)
        with dve.Fori(0, DEPTH) as layer:
            dve.wait_ge(layer_go, layer + 1)
            dve.nop(nofuse=True)
            dve.sem_inc(sc_hi, 1)
            dve.sem_inc(ff_hi, 1)
            dve.wait_ge(par_landed, 16)
            step = Steps(dve, dve_step)

            def rms(name, src, gain):
                base = RMS_BASE[name]
                dve.wait_ge(root_done, list(RMS_BASE).index(name) + 1)
                step(v.reciprocal(RSTD[:, :], RSTD[:, :]))
                for k in range(RMS_TILES[name]):
                    if base + k >= 2:
                        dve.wait_ge(n_lo, base + k - 1)
                    v.scalar_tensor_tensor(T[:, k % 2, :], src(k), par(gain + k), RSTD[:, :], ALU.mult, ALU.mult)\
                        .then_inc(t_done, 1)

            def taps(acc, src, col, offsets, last=None):
                for m, (tap, o) in enumerate(offsets):
                    lo, hi = max(0, -o), SEQ - max(0, o)
                    ins = v.scalar_tensor_tensor(acc[:, lo:hi], src[:, lo + o:hi + o], par(col + tap), acc[:, lo:hi],
                                                 ALU.mult, ALU.add)
                    if last is not None and m == len(offsets) - 1:
                        ins.then_inc(last, 1)
                    else:
                        step(ins)

            rms("norm1", lambda k: X[:, k, :], PA_N1)
            seven = [(tap, tap - SSD_TAPS // 2) for tap in range(SSD_TAPS) if tap != SSD_TAPS // 2]
            with dve.Fori(0, 6) as i:
                step.enter(i, 10)
                for b in range(2):
                    dve.wait_ge(tap_first, i * 2 + (b + 1))
                    taps(ACC7[:, b, :], bank(b), i * 16 + (PA_CONV7 + 8 * b), seven, last=evac[b])
                step.leave(6)
            for n in range(8):
                dve.wait_ge(evac[n % 2], (N_QK + n) // 2 + 1)
                src = tile_of((Q, K)[n // 4], n % 4)
                v.tensor_tensor(QKSQ[:, n, :], src, src, ALU.mult).then_inc(qk_sq, 1)
            for n in range(8):
                dve.wait_ge(qk_root, n + 1)
                step(v.reciprocal(QKSQ[:, n, :], QKSQ[:, n, :]))
                src = tile_of((Q, K)[n // 4], n % 4)
                v.scalar_tensor_tensor(src, src, par((PA_QG, PA_KG)[n // 4]), QKSQ[:, n, :], ALU.mult, ALU.mult)\
                    .then_inc(qk_norm, 1)
            with dve.Fori(0, 2) as i:
                step.enter(i, 4)
                for j in range(6):
                    b, t = j % 2, i * 2 + j // 3
                    if j % 3 == 1:
                        dve.wait_ge(w_used, i * 6 + (C_SC + j + 1))
                        dve.wait_ge(evac[1 - b], i * 3 + ((N_SC + j - 1) // 2 + 1))
                        v.tensor_tensor(CX[:, :], bank(b), SCC[:, :], ALU.mult).then_inc(evac[b], 1)
                        dve.wait_ge(cx_tap, t + 1)
                        taps(SCA, CX, t * 4 + PA_SC, [(0, -1), (2, 1)])
                    if j % 3 == 2:
                        dve.wait_ge(w_used, i * 6 + (C_SC + j + 1))
                        dve.wait_ge(sc_lo, t + 1)
                        v.tensor_tensor(SCP[:, :], bank(b), SCA[:, :], ALU.mult).then_inc(evac[b], 1)
                        dve.wait_ge(evac[b], i * 3 + ((N_SC + j) // 2 + 1))
                        v.tensor_copy(tile_of(o2["mh_sc"], t), SCP[:, :]).then_inc(sc_hi, 1)
                step.leave(2)

            dve.wait_ge(w_used, C_OUT)
            for c in range(QT):
                step(v.tensor_tensor(SM[:, 0, 64 * c:64 * c + 64], BANK[:, 2 + c, 0:64], par(PA_DTB, 64), ALU.add))
            dtf = DT[:, :, :].rearrange("p c n -> p (c n)")
            daf = DA[:, :, :].rearrange("p c n -> p (c n)")
            step(v.tensor_scalar(dtf, SM[:, 0, :], 0.0, None, ALU.max))
            step(v.tensor_scalar(SM[:, 1, :], SM[:, 0, :], 0.0, None, ALU.min))
            v.tensor_tensor(SM[:, 1, :], SM[:, 1, :], dtf, ALU.subtract).then_inc(dt_x, 1)
            dve.wait_ge(dt_e, 1)
            v.tensor_scalar(SM[:, 2, :], SM[:, 1, :], 1.0, None, ALU.add).then_inc(dt_w, 1)
            dve.wait_ge(dt_w, 1)
            step(v.tensor_scalar(SM[:, 0, :], SM[:, 2, :], 1.0, None, ALU.subtract))
            step(v.tensor_scalar(daf, SM[:, 0, :], 0.0, None, ALU.is_equal))
            step(v.tensor_tensor(SM[:, 0, :], SM[:, 0, :], daf, ALU.add))
            step(v.reciprocal(SM[:, 0, :], SM[:, 0, :]))
            dve.wait_ge(dt_ln, 1)
            step(v.tensor_tensor(SM[:, 3, :], SM[:, 3, :], daf, ALU.add))
            step(v.tensor_tensor(SM[:, 3, :], SM[:, 3, :], SM[:, 0, :], ALU.mult))
            step(v.tensor_tensor(SM[:, 3, :], SM[:, 3, :], SM[:, 1, :], ALU.mult))
            step(v.tensor_tensor(dtf, dtf, SM[:, 3, :], ALU.add))
            dve.wait_ge(a_exp, 1)
            v.scalar_tensor_tensor(DA[:, :, :], DT[:, :, :], -1.0, par(PA_ALOG, 64).unsqueeze(1).to_broadcast([P, QT, 64]),
                                   ALU.mult, ALU.mult).then_inc(da_done, 1)

            def at_neg_max(u):
                h, qt = u // 4, u % 4
                dve.wait_ge(at_qk, u + 1)
                dve.wait_ge(bias_landed[h % 2], 16 * (h // 2 + 1))
                if u >= 2:
                    dve.wait_ge(at_exp, u - 1)
                at = SEQ - P - P * qt
                v.tensor_tensor_reduce(S[:, u % 2, :], bank(2 + u % 2), BIAS[:, h % 2, at:at + SEQ], scale=-1.0, scalar=3e38,
                                       op0=ALU.add, op1=ALU.min, accum_out=NEGMAX[:, u % 4:u % 4 + 1]).then_inc(at_neg, 1)

            def at_normalize(u):
                dve.wait_ge(at_exp, u + 1)
                col = slice(u % 4, u % 4 + 1)
                step(v.reciprocal(RDEN[:, col], DEN[:, col]))
                v.tensor_scalar(PR[:, u % 2, :], PR[:, u % 2, :], RDEN[:, col], None, ALU.mult).then_inc(at_p, 1)

            def at_low(t):
                dve.wait_ge(at_hi, t + 1)
                v.tensor_tensor(o2["ml_at"][:, t, :], bank(6 + t % 2), o2["mh_at"][:, t, :].bitcast(F32), ALU.subtract)\
                    .then_inc(at_lo, 1)

            at_neg_max(0)
            for u in range(4 * HEADS):
                if u + 1 < 4 * HEADS:
                    at_neg_max(u + 1)
                at_normalize(u)
                if u % 8 == 4 and u > 8:
                    at_low(u // 8 - 1)
            at_low(HEADS // 2 - 1)

            dve.wait_ge(cs_hi, 1)
            v.tensor_tensor(CSLO[0:64, :], BANK[0:64, 2, :], CSHI[0:64, :].bitcast(F32), ALU.subtract).then_inc(cs_lo, 1)
            dve.wait_ge(dec_exp, 1)
            v.tensor_tensor(WS[:, :, :], EW[:, :, 0:64], DT[:, :, :], ALU.mult).then_inc(ws_done, 1)
            dve.wait_ge(cs_col, 1)

            def chunks(x):
                return x.rearrange("p (c l) -> p c l", l=P)

            def seg(h):
                for d in range(2):
                    dve.wait_ge(ab_mm, 2 * h + d + 1)
                    if h >= 2:
                        dve.wait_ge(y_mm, h - 1)
                    col = column(d, h)
                    v.tensor_tensor(chunks(E[:, d, h % 2, :]), chunks(bank(2 + 2 * (h % 2) + d)),
                                    AS[:, :, col:col + 1].to_broadcast([P, QT, P]), ALU.subtract).then_inc(seg_done, 1)

            def weigh(h):
                for d in range(2):
                    dve.wait_ge(e_done, 2 * h + d + 1)
                    for c in range(QT):
                        at = slice(P * c, P * c + P)
                        ins = v.scalar_tensor_tensor(E[:, d, h % 2, at], E[:, d, h % 2, at], DT[:, c, column(d, h):column(d, h) + 1],
                                                     CB[:, d, at], ALU.mult, ALU.mult)
                ins.then_inc(g_done, 1)

            def combine(t):
                dve.wait_ge(y_mm, 2 * t + 2)
                step(v.scalar_tensor_tensor(XC[:, t, :], XC[:, t, :], par(PA_D + t), bank(6 + t % 2), ALU.mult, ALU.add))
                dve.wait_ge(yo_mm, t + 1)
                dve.wait_ge(ea_done, 4 * t + 4)
                spans = (slice(P, SEQ), slice(0, SEQ - P))
                for d in range(2):
                    step(v.tensor_tensor(T[:, d, spans[d]], BANK[:, d, spans[d]], EA[:, d, t % 2, spans[d]], ALU.mult))
                for d in range(2):
                    step(v.tensor_tensor(XC[:, t, spans[d]], XC[:, t, spans[d]], T[:, d, spans[d]], ALU.add))
                v.tensor_tensor(Z[:, t, :], Z[:, t, :], XC[:, t, :], ALU.mult).then_inc(y_comb, 1)

            for grp in range(SSD_GROUPS):
                dve.wait_ge(cb_mm, grp + 1)
                for d in range(2):
                    v.tensor_tensor(chunks(CB[:, d, :]), chunks(bank(6)),
                                    con[("le", "ge")[d]].unsqueeze(1).to_broadcast([P, QT, P]), ALU.mult).then_inc(cb_done, 1)
                dve.wait_ge(cb_done, 2 * grp + 2)
                for j in range(6):
                    (d, c), i, n = direction_chunk(j), j // 2, 6 * grp + j
                    if i == 0:
                        dve.wait_ge(st_mm, n + 1)
                        v.tensor_copy(SIN[:, d, 0, :], bank(j % 2)).then_inc(sin_done, 1)
                        continue
                    if grp:
                        dve.wait_ge(n_lo, RMS_BASE["ssd1"])
                    col = 64 + column(d, 8 * grp)
                    dve.wait_ge(sin_done, n - 1)
                    step(v.tensor_tensor(T[:, d, :].rearrange("p (h e) -> p h e", e=64),
                                         SIN[:, d, i - 1, :].rearrange("p (h e) -> p h e", e=64),
                                         EW[:, c, col:col + 8].unsqueeze(2).to_broadcast([P, 8, 64]), ALU.mult))
                    dve.wait_ge(st_mm, n + 1)
                    v.tensor_tensor(SIN[:, d, i, :], bank(j % 2), T[:, d, :], ALU.add).then_inc(sin_done, 1)
                h0 = 8 * grp
                seg(h0)
                for hh in range(8):
                    if hh < 7:
                        seg(h0 + hh + 1)
                    weigh(h0 + hh)
                    if hh % 2 == 0 and hh:
                        combine((h0 + hh) // 2 - 1)
                combine(4 * grp + 3)
                rms(f"ssd{grp}", lambda k: Z[:, 4 * grp + k, :], PA_SNG + 4 * grp)

            for m in range(KT):
                dve.wait_ge(w_used, C_OUT + 2 * m + 2)
                v.tensor_tensor(X[:, m, :], bank(m % 2), X[:, m, :], ALU.add).then_inc(x_added, 1)
            rms("norm2", lambda k: X[:, k, :], PA_N2)
            with dve.Fori(0, FF_T // 2) as i:
                step.enter(i, 6)
                for j in range(4):
                    b, pb, t = j % 2, j // 2, i * 2 + j // 2
                    dve.wait_ge(ff_tap, i * 4 + (j + 1))
                    taps((FG, FV)[b][:, pb, :], bank(b), i * 16 + (PA_FF + 4 * j), [(0, -1), (2, 1)], last=evac[b])
                    if b == 1:
                        dve.wait_ge(evac[b], t + (N_UP // 2 + 1))
                        dve.wait_ge(ff_silu, t + 1)
                        dve.wait_ge(ff_lo, t + 1)
                        step(v.tensor_tensor(FP[:, :], FS[:, :], FV[:, pb, :], ALU.mult))
                        v.tensor_copy(tile_of(FHI, t), FP[:, :]).then_inc(ff_hi, 1)
                step.leave(FF_T // 2)
            with dve.Fori(0, KT // 2) as i:
                for b in range(2):
                    dve.wait_ge(w_used, i * (2 * DOWN_C) + (C_DOWN + DOWN_C * (b + 1)))
                    v.tensor_tensor(tile_of(X, i * 2 + b), bank(b), tile_of(X, i * 2 + b), ALU.add).then_inc(evac[b], 1)
            dve.drain().then_inc(layer_end, 1)

    @block.tensor
    def _(pe):
        mm, transpose = nc.tensor.matmul, nc.tensor.transpose

        pe.wait_ge(setup_landed, 48)
        for r in range(2):
            mm(BANK[0:HEADS, r, :], o2["table"][:, :], o2["onehot"][:, 512 * r:512 * r + 512], start=True, stop=True)\
                .then_inc(bias_mm, 1)
        pe.wait_ge(con_landed, 16)
        pe.wait_ge(idr_done, 1)

        def products(out, blocks, start, stop):
            for k, (whi, wlo, hhi, hlo) in enumerate(blocks):
                for p, (l, r) in enumerate(((whi, hhi), (whi, hlo), (wlo, hhi))):
                    ins = mm(out, l, r, start=start and k == 0 and p == 0, stop=stop and k == len(blocks) - 1 and p == 2)
            return ins

        def chunk_blocks(b, hs, n=KT):
            at = [slice(P * k, P * k + P) for k in range(n)]
            return [(WHI[:, b, at[k]], WLO[:, b, at[k]], *hs(k)) for k in range(n)]

        def normed(k):
            return HHI[:, k, :], HLO[:, k, :]

        def tiles(c0, n0, count):
            with pe.Fori(0, count // 2) as i:
                for b in range(2):
                    pe.wait_ge(w_lo, i * 2 + (c0 + b + 1))
                    if n0:
                        pe.wait_ge(evac[b], i + n0 // 2)
                    products(bank(b), chunk_blocks(b, normed), True, True).then_inc(w_used, 1)

        def rms(name, before=None):
            base, n = RMS_BASE[name], RMS_TILES[name]
            if before is not None:
                before()
            for k in range(n):
                pe.wait_ge(sq_done, base + k + 1)
                mm(rms_bank(name), con["ones"], SQ[:, k % 2, :], start=k == 0, stop=k == n - 1).then_inc(ss_done, 1)

        with pe.Fori(0, DEPTH) as layer:
            pe.wait_ge(layer_go, layer + 1)
            pe.nop(nofuse=True)
            rms("norm1")
            pe.wait_ge(n_lo, KT)
            for b in range(2):
                pe.wait_ge(w_lo, b + 1)
                products(bank(b), chunk_blocks(b, normed), True, True).then_inc(w_used, 1)
            tiles(2, 2, C_QK - 2)
            tiles(C_QK, N_QK, 8)
            for j in range(4):
                pe.wait_ge(w_lo, C_V + j + 1)
                for c in range(QT):
                    at = slice(P * c, P * c + P)
                    blocks = [(HHI[:, 2 * j + k, at], HLO[:, 2 * j + k, at], WHI[:, j % 2, 512 * k:512 * k + 512],
                               WLO[:, j % 2, 512 * k:512 * k + 512]) for k in range(2)]
                    ins = products(bank(2 + c), blocks, j == 0, j == 3)
                ins.then_inc(w_used, 1)
            for n in range(8):
                pe.wait_ge(qk_sq, n + 1)
                if n >= 2:
                    pe.wait_ge(qk_root, n - 1)
                mm(bank(6 + n % 2), con["headones"], QKSQ[:, n, :], start=True, stop=True).then_inc(qk_ss, 1)
            tiles(C_Z, N_Z, 8)
            tiles(C_SC, N_SC, 12)
            pe.wait_ge(v_copied, QT)
            for j in range(2):
                pe.wait_ge(w_lo, C_DT + j + 1)
                for c in range(QT):
                    at = slice(P * c, P * c + P)
                    blocks = [(HHI[:, 4 * j + k, at], HLO[:, 4 * j + k, at], WHI[:, j, 64 * k:64 * k + 64],
                               WLO[:, j, 64 * k:64 * k + 64]) for k in range(4)]
                    ins = products(BANK[:, 2 + c, 0:64], blocks, j == 0, j == 1)
                ins.then_inc(w_used, 1)

            def qk(u):
                h, qt = u // 4, u % 4
                hs = slice(64 * (h % 2), 64 * (h % 2) + 64)
                if u >= 2:
                    pe.wait_ge(at_neg, u - 1)
                mm(bank(2 + u % 2), Q[hs, h // 2, P * qt:P * qt + P], K[hs, h // 2, :], start=True, stop=True)\
                    .then_inc(at_qk, 1)

            def turn(u):
                pe.wait_ge(at_p, u + 1)
                if u >= 2:
                    pe.wait_ge(at_ptc, u - 1)
                for j in range(QT):
                    ins = transpose(BANK[:, 4 + u % 2, P * j:P * j + P], PR[:, u % 2, P * j:P * j + P], con["ident"])
                ins.then_inc(at_tr, 1)

            def pv(h):
                t, half = h // 2, 64 * (h % 2)
                pe.wait_ge(at_ptc, 4 * h + 4)
                if t >= 2:
                    pe.wait_ge(at_lo, t - 1)
                for j in range(QT):
                    ins = mm(BANK[half:half + 64, 6 + t % 2, :], V[:, j, 64 * h:64 * h + 64], PTS[:, h % 2, j, :],
                             start=j == 0, stop=j == QT - 1)
                ins.then_inc(at_pv, 1)

            pe.wait_ge(qk_norm, 8)
            pe.wait_ge(dt_x, 1)
            qk(0)
            qk(1)
            for u in range(4 * HEADS):
                turn(u)
                if u + 2 < 4 * HEADS:
                    qk(u + 2)
                if u % 4 == 1 and u > 4:
                    pv(u // 4 - 1)
            pv(HEADS - 1)

            pe.wait_ge(da_done, 1)
            pe.wait_ge(at_lo, HEADS // 2)
            for c in range(QT):
                for d in range(2):
                    ins = mm(BANK[DIR * d:DIR * d + DIR, 2, P * c:P * c + P], DA[:, c, DIR * d:DIR * d + DIR],
                             con[("le", "ge")[d]], start=True, stop=True)
            ins.then_inc(cs_mm, 1)
            for c in range(QT):
                for d in range(2):
                    mm(BANK[:, 4, P * c + DIR * d:P * c + DIR * d + DIR], con[("gt", "lt")[d]],
                       DA[:, c, DIR * d:DIR * d + DIR], start=True, stop=True)
                ins = mm(BANK[:, 4, P * c + 64:P * c + P], con["ones"], DA[:, c, :], start=True, stop=True)
            ins.then_inc(dec_mm, 1)
            pe.wait_ge(cs_row, 1)
            for c in range(QT):
                ins = transpose(BANK[:, 3, 64 * c:64 * c + 64], T[0:64, 0, P * c:P * c + P], con["ident"][0:64, 0:64])
            ins.then_inc(cs_tr, 1)
            for n in range(10):
                if n >= 2:
                    pe.wait_ge(tok_copied, n - 1)
                for m in range(4):
                    if n < 8:
                        src = XC[:, 4 * (n % 2) + m, P * (n // 2):P * (n // 2) + P]
                    else:
                        c = 2 * (n - 8) + m // 2
                        src = BC[:, m % 2, P * c:P * c + P]
                    ins = transpose(BANK[:, 5 + n % 2, P * m:P * m + P], src, con["ident"])
                ins.then_inc(tok_tr, 1)

            def row_sums(h):
                if h >= 2:
                    pe.wait_ge(seg_done, 2 * h - 2)
                    pe.wait_ge(ea_done, 2 * h - 2)
                for d in range(2):
                    row = IDR[0:64, column(d, h):column(d, h) + 1].to_broadcast([64, P])
                    mm(bank(2 + 2 * (h % 2) + d), row, CSHI[0:64, :], start=True, stop=False)
                    mm(bank(2 + 2 * (h % 2) + d), row, CSLO[0:64, :], start=False, stop=True).then_inc(ab_mm, 1)

            def within(h):
                t, half, grp = h // 2, 64 * (h % 2), h // 8
                pe.wait_ge(gs_done, h + 1)
                if t >= 2:
                    pe.wait_ge(y_comb, t - 1)
                for c in range(QT):
                    ins = mm(BANK[half:half + 64, 6 + t % 2, P * c:P * c + P], XT[:, c, 64 * h:64 * h + 64],
                             E[:, 0, h % 2, P * c:P * c + P], start=True, stop=True)
                ins.then_inc(y_mm, 1)

            def from_states(t):
                grp, at = t // 4, slice(P * (t % 4), P * (t % 4) + P)
                pe.wait_ge(y_comb, t) if t else None
                for i in range(QT - 1):
                    for d in range(2):
                        c = i + 1 if d == 0 else QT - 2 - i
                        ins = mm(BANK[:, d, P * c:P * c + P], SIN[:, d, i, at], BC[:, 2 + grp, P * c:P * c + P],
                                 start=True, stop=True)
                ins.then_inc(yo_mm, 1)

            pe.wait_ge(cs_lo, 1)
            pe.wait_ge(cs_col, 1)
            pe.wait_ge(dec_exp, 1)
            for grp in range(SSD_GROUPS):
                pe.wait_ge(tok_copied, 10)
                if grp:
                    pe.wait_ge(y_comb, 4 * grp)
                for c in range(QT):
                    at = slice(P * c, P * c + P)
                    ins = mm(BANK[:, 6, at], BC[:, grp, at], BC[:, 2 + grp, at], start=True, stop=True)
                ins.then_inc(cb_mm, 1)
                if grp:
                    pe.wait_ge(root_done, 1 + grp)
                for j in range(6):
                    d, c = direction_chunk(j)
                    n = 6 * grp + j
                    pe.wait_ge(xs_done, n + 1)
                    if j >= 2:
                        pe.wait_ge(sin_done, n - 1)
                    mm(bank(j % 2), BT[:, c, P * grp:P * grp + P], XS[:, j % 2, :], start=True, stop=True).then_inc(st_mm, 1)
                pe.wait_ge(cb_done, 2 * grp + 2)
                pe.wait_ge(sin_done, 6 * grp + 6)
                row_sums(8 * grp)
                for hh in range(8):
                    h = 8 * grp + hh
                    if hh < 7:
                        row_sums(h + 1)
                    if hh % 2 == 0:
                        from_states(h // 2)
                    within(h)
                rms(f"ssd{grp}", lambda: pe.wait_ge(y_comb, 4 * grp + 4))

            pe.wait_ge(n_lo, RMS_BASE["norm2"])
            pe.wait_ge(sc_lo, 5)
            pe.wait_ge(at_lo, 4)
            for m in range(KT):
                if m >= 2:
                    pe.wait_ge(x_added, m - 1)
                for j in range(2):
                    pe.wait_ge(w_lo, C_OUT + 2 * m + j + 1)
                    products(bank(m % 2), chunk_blocks(j, lambda k: (mixed("h", 8 * j + k), mixed("l", 8 * j + k))),
                             j == 0, j == 1).then_inc(w_used, 1)
            rms("norm2")
            pe.wait_ge(n_lo, RMS_BASE["norm2"] + KT)
            tiles(C_UP, N_UP, 2 * FF_T)
            pe.wait_ge(ff_lo, FF_T + 1)
            with pe.Fori(0, KT // 2) as i:
                for b in range(2):
                    pe.wait_ge(evac[b], i + N_DOWN // 2)
                    for j in range(DOWN_C):
                        s = (DOWN_C * b + j) % 2
                        pe.wait_ge(w_lo, i * (2 * DOWN_C) + (C_DOWN + DOWN_C * b + j + 1))
                        n = min(KT, FF_T - KT * j)
                        products(bank(b), chunk_blocks(s, lambda k: (FHI[:, KT * j + k, :], FLO[:, KT * j + k, :]), n),
                                 j == 0, j == DOWN_C - 1).then_inc(w_used, 1)
            pe.drain().then_inc(layer_end, 1)

    ctx.close()


def _blocks(w, n_blocks):
    layers, rows, cols = w.shape
    k = rows // P
    chunks = -(-k // n_blocks)
    b = w.reshape(layers, k, P, cols // P, P).transpose(0, 3, 2, 1, 4)
    if chunks * n_blocks != k:
        b = np.concatenate([b, np.zeros(b.shape[:3] + (chunks * n_blocks - k, P), b.dtype)], axis=3)
    b = b.reshape(layers, cols // P, P, chunks, n_blocks * P).transpose(0, 1, 3, 2, 4)
    return np.ascontiguousarray(b.reshape(layers, cols // P * chunks, P, n_blocks * P))


def _bias_constants():
    rel = np.arange(REL) - (SEQ - 1)
    n = np.abs(rel)
    nb = BUCKETS // 2
    exact = nb // 2
    large = exact + (np.log(np.maximum(n, 1).astype(np.float32) / exact) / math.log(MAX_DISTANCE / exact)
                     * (nb - exact)).astype(np.int32)
    bucket = np.where(rel > 0, nb, 0) + np.where(n < exact, n, np.minimum(large, nb - 1))
    onehot = (np.arange(BUCKETS)[:, None] == bucket[None, :]).astype(np.float32)
    count = sum(((n % d == 0) & (n // d <= w // 2 // d)).astype(np.int32) for w, d in PATTERNS)
    log_count = np.where(count > 0, np.log(np.maximum(count, 1)), NEG).astype(np.float32)
    return onehot, np.ascontiguousarray(np.broadcast_to(log_count, (HEADS, REL)))


def _constants():
    i, j = np.arange(P)[:, None], np.arange(P)[None, :]
    made = {"ident": i == j, "ones": i >= 0 * j, "le": i <= j, "ge": i >= j, "gt": i > j, "lt": i < j,
            "headones": i // HEAD_DIM == j // HEAD_DIM}
    return np.ascontiguousarray(np.stack([made[n] for n in CONSTS], axis=1).astype(np.float32))


def kernel(x, rel_table, norm1_g, w_in, q_norm_g, k_norm_g, ssd_conv_w, ssd_conv_b, ssd_dt_bias, ssd_a_log, ssd_d,
           ssd_norm_g, sc_conv_w, sc_conv_b, w_out, norm2_g, ffn_w_up, ffn_conv_w, ffn_conv_b, ffn_w_down):
    import concourse.bacc as bacc
    from concourse.bass_utils import run_bass_kernel_spmd

    f = np.asarray
    w = f(w_in)
    ends = np.cumsum([512, 512, 512, 1024, 1536, 32, 512, 512, 512])
    wq, wk, wv, wz, wx, wdt, wb, wc, wxin = np.split(w, ends[:-1], axis=2)
    v_chunks = wv.reshape(DEPTH, 4, 2, P, 512).transpose(0, 1, 3, 2, 4).reshape(DEPTH, 4, P, CHUNK)
    sc = np.stack([_blocks(m, KT) for m in (wc, wxin, wb)], axis=2).reshape(DEPTH, 12, P, CHUNK)
    win = np.concatenate([_blocks(wx, KT), _blocks(wq, KT), _blocks(wk, KT), v_chunks, _blocks(wz, KT), sc], axis=1)

    def padded(m):
        m = m.reshape(m.shape[:-1] + (2, SSD_HEADS))
        m = np.concatenate([m, np.zeros(m.shape[:-1] + (DIR - SSD_HEADS,), m.dtype)], axis=-1)
        return m.reshape(m.shape[:-2] + (2 * DIR,))

    wd = padded(wdt).reshape(DEPTH, 2, 4, P, 64).transpose(0, 1, 3, 2, 4).reshape(DEPTH * 2, P, 256)
    up = np.stack(np.split(_blocks(f(ffn_w_up), KT), 2, axis=1), axis=2)

    def columns(m):
        return m.reshape(DEPTH, m.shape[1], -1, P).transpose(0, 3, 2, 1)

    def rows(m):
        return np.broadcast_to(m[:, None, :], (DEPTH, P, m.shape[-1]))

    conv7 = columns(np.concatenate([f(ssd_conv_w), f(ssd_conv_b)[:, None]], axis=1))
    conv_sc = columns(np.concatenate([f(sc_conv_w), f(sc_conv_b)[:, None]], axis=1))
    conv_ff = columns(np.concatenate([f(ffn_conv_w), f(ffn_conv_b)[:, None]], axis=1))
    conv_ff = np.stack(np.split(conv_ff, 2, axis=2), axis=3)
    params = np.concatenate([p.reshape(DEPTH, P, -1) for p in (
        columns(f(norm1_g)[:, None]), columns(f(norm2_g)[:, None]),
        np.concatenate([f(q_norm_g)] * 2, axis=1)[:, :, None], np.concatenate([f(k_norm_g)] * 2, axis=1)[:, :, None],
        conv7, columns(np.repeat(f(ssd_d), SSD_W // SSD_HEADS, axis=1)[:, None]), columns(f(ssd_norm_g)[:, None]),
        conv_sc, conv_ff,
        rows(padded(f(ssd_dt_bias).reshape(DEPTH, 32))), rows(padded(f(ssd_a_log).reshape(DEPTH, 32))),
    )], axis=2)
    assert params.shape[2] == PA_N
    onehot, log_count = _bias_constants()
    arrays = {
        "constants": _constants(), "x_t": f(x)[0].T, "onehot": onehot, "log_count": log_count,
        "rel_table": f(rel_table), "params": params,
        "w_in": win.reshape(-1, P, CHUNK), "w_dt": wd,
        "w_out": _blocks(f(w_out), KT).reshape(-1, P, CHUNK),
        "w_up": up.reshape(-1, P, CHUNK),
        "w_down": _blocks(f(ffn_w_down), KT).reshape(-1, P, CHUNK),
    }
    arrays = {n: np.ascontiguousarray(m) for n, m in arrays.items()}
    nc = bacc.Bacc("TRN2", target_bir_lowering=False, num_devices=1)
    aps = {n: nc.dram_tensor(n, m.shape, mybir.dt.from_np(m.dtype), kind="ExternalInput").ap() for n, m in arrays.items()}
    aps["out_t"] = nc.dram_tensor("out_t", (D_MODEL, SEQ), F32, kind="ExternalOutput").ap()
    build_trunk(nc, aps)
    r = run_bass_kernel_spmd(nc, [arrays], core_ids=[0])
    return np.ascontiguousarray(r.results[0]["out_t"].T)[None]
```

```python
import math
from contextlib import ExitStack

import numpy as np

import concourse.bass as bass
from concourse import mybir

F32, F32R = mybir.dt.float32, mybir.dt.float32r
ACT, ALU = mybir.ActivationFunctionType, mybir.AluOpType
P = 128

D_MODEL, SEQ, DEPTH = 1024, 512, 2
HEADS, HEAD_DIM = 8, 64
PATTERNS = ((128, 1), (512, 4), (2048, 16))
BUCKETS, MAX_DISTANCE = 32, 1024
SSD_HEADS, SSD_GROUPS = 16, 2
SSD_TAPS, D_FF = 7, 2816
EPS, NEG = 1e-6, -1e30
ATTN_W, SSD_W, SC_W = 512, 1024, 512

KT = D_MODEL // P
QT = SEQ // P
CHUNK = KT * P
FF_T = D_FF // P
DOWN_C = -(-FF_T // KT)
DIR = 32
REL = 2 * SEQ
TOEP = 2 * SEQ - P

C_XBC, C_QK, C_V, C_Z, C_SC = 0, 12, 20, 24, 32
C_DT, C_OUT = 44, 46
C_UP = C_OUT + 2 * KT
C_DOWN = C_UP + 2 * FF_T
C_END = C_DOWN + DOWN_C * KT
N_IN = C_DT
N_XBC, N_QK, N_Z, N_SC = 0, 12, 20, 28
N_OUT = 40
N_UP = N_OUT
N_DOWN = N_UP + 2 * FF_T

_at = 0


def _cols(n):
    global _at
    _at += n
    return _at - n


PA_N1, PA_N2, PA_QG, PA_KG = _cols(KT), _cols(KT), _cols(1), _cols(1)
PA_CONV7, PA_D, PA_SNG = _cols(12 * 8), _cols(8), _cols(8)
PA_SC, PA_FF = _cols(4 * 4), _cols(2 * FF_T * 4)
PA_DTB, PA_ALOG = _cols(64), _cols(64)
PA_N = _at

CONSTS = ("ident", "ones", "le", "ge", "gt", "lt", "headones")
RMS_BASE = {"norm1": 0, "ssd0": 8, "ssd1": 12, "norm2": 16}
RMS_TILES = {"norm1": KT, "ssd0": 4, "ssd1": 4, "norm2": KT}


OUT_ORDER = [(m, j) for j in range(2) for m in range(6)] + [(m, j) for m in (6, 7) for j in range(2)]


OUT_ENDS = {OUT_ORDER.index((m, 1)): m for m in range(8)}


class Steps:

    def __init__(self, eng, sem):
        self.eng, self.sem, self.n, self.turn = eng, sem, 0, None

    def __call__(self, ins):
        ins.then_inc(self.sem, 1)
        self.n += 1
        self.eng.wait_ge(self.sem, self.value())

    def value(self):
        return self.n if self.turn is None else self.turn[0] * self.turn[1] + self.n

    def enter(self, turn, per_turn):
        self.turn, self.start = (turn, per_turn), self.n

    def leave(self, turns):
        per_turn = self.turn[1]
        assert self.n - self.start == per_turn, (self.n - self.start, per_turn)
        self.turn, self.n = None, self.start + turns * per_turn


def build_trunk(nc, a):
    ctx = ExitStack()

    def sb(name, shape, dt=F32):
        return ctx.enter_context(nc.sbuf_tensor(f"sb_{name}", shape, dt))

    def sem(name):
        return ctx.enter_context(nc.semaphore(name))

    def overlay(name, *groups):
        found, most = {}, 0
        for group in groups:
            size = 0
            with ExitStack() as st:
                for n, shape, dt in group:
                    found[n] = st.enter_context(nc.sbuf_tensor(f"sb_{n}", shape, dt))
                    size += 4 * math.prod(shape[1:])
            most = max(most, size)
        sb(name, [P, most // 4])
        return found

    X = sb("x_stream", [P, KT, SEQ])
    CON = sb("constants", [P, len(CONSTS), P])
    con = {n: CON[:, i, :] for i, n in enumerate(CONSTS)}
    IDR = sb("ident_r", [P, P], F32R)
    PAR = sb("params", [P, PA_N])
    EPSC = sb("eps_columns", [P, 2])
    W = sb("w_raw", [P, 2, CHUNK])
    WHI = sb("w_hi", [P, 2, CHUNK], F32R)
    WLO = sb("w_lo", [P, 2, CHUNK], F32R)
    T = sb("t_normed", [P, 2, SEQ])
    SQ = sb("squares", [P, 2, SEQ])
    RSTD = sb("rstd", [P, SEQ])
    DT = sb("dt", [P, QT, 64])
    DA = sb("dt_a", [P, QT, 64])
    SM = sb("small", [P, 4, QT * 64])
    EW = sb("decays", [P, QT, P])
    WS = sb("state_weights", [P, QT, 64])
    AS = sb("cumsum_columns", [P, QT, 64])
    NEGMAX = sb("neg_max", [P, 4])
    DEN = sb("softmax_sums", [P, 4])
    RDEN = sb("softmax_recips", [P, 4])

    o1 = overlay(
        "region_h",
        [("h_hi", [P, KT, SEQ], F32R), ("h_lo", [P, KT, SEQ], F32R)],
        [("probs_t", [P, 2, QT, SEQ], F32), ("bias_t", [P, 2, TOEP], F32)],
        [("x_tok", [P, QT, SSD_W], F32), ("b_tok", [P, QT, 256], F32), ("cs_hi", [P, SEQ], F32R),
         ("cs_lo", [P, SEQ], F32R), ("exp_cs", [P, 2, 2, SEQ], F32)],
    )
    HHI, HLO = o1["h_hi"], o1["h_lo"]
    PTS, BIAS = o1["probs_t"], o1["bias_t"]
    XT, BT, CSHI, CSLO, EA = (o1[n] for n in ("x_tok", "b_tok", "cs_hi", "cs_lo", "exp_cs"))
    o2 = overlay(
        "region_m",
        [("ff_hi", [P, FF_T, SEQ], F32R), ("ff_lo", [P, FF_T, SEQ], F32R), ("ff_gate", [P, 2, SEQ], F32),
         ("ff_val", [P, 2, SEQ], F32), ("ff_silu", [P, SEQ], F32), ("ff_prod", [P, SEQ], F32)],
        [("mh_ssd", [P, 8, SEQ], F32R), ("ml_ssd", [P, 8, SEQ], F32R), ("mh_at", [P, 4, SEQ], F32R),
         ("ml_at", [P, 4, SEQ], F32R), ("mh_sc", [P, 4, SEQ], F32R), ("ml_sc", [P, 4, SEQ], F32R)],
        [("z", [P, 8, SEQ], F32), ("xc", [P, 8, SEQ], F32), ("q", [P, 4, SEQ], F32), ("k", [P, 4, SEQ], F32),
         ("qk_sq", [P, 8, SEQ], F32), ("bc", [P, 4, SEQ], F32), ("v", [P, QT, ATTN_W], F32),
         ("conv_acc", [P, 2, SEQ], F32), ("sc_c", [P, SEQ], F32), ("sc_cx", [P, SEQ], F32),
         ("sc_acc", [P, SEQ], F32), ("sc_prod", [P, SEQ], F32)],
        [("pad_a", [P, 36, SEQ], F32), ("cb", [P, 2, SEQ], F32), ("s_in", [P, 2, 3, SEQ], F32),
         ("x_scaled", [P, 2, SEQ], F32), ("e", [P, 2, 2, SEQ], F32), ("g", [P, 2, SEQ], F32)],
        [("pad_b", [P, 40, SEQ], F32), ("scores", [P, 2, SEQ], F32), ("probs", [P, 2, SEQ], F32)],
        [("pad_c", [P, 42, SEQ], F32), ("onehot", [BUCKETS, REL], F32), ("log_count", [HEADS, REL], F32), ("table", [BUCKETS, HEADS], F32),
         ("bias_row", [HEADS, REL], F32)],
    )
    FHI, FLO, FG, FV, FS, FP = (o2[n] for n in ("ff_hi", "ff_lo", "ff_gate", "ff_val", "ff_silu", "ff_prod"))
    Z, XC, Q, K, QKSQ, BC, V = (o2[n] for n in ("z", "xc", "q", "k", "qk_sq", "bc", "v"))
    ACC7, SCC, CX, SCA, SCP = (o2[n] for n in ("conv_acc", "sc_c", "sc_cx", "sc_acc", "sc_prod"))
    CB, SIN, XS, E, G = (o2[n] for n in ("cb", "s_in", "x_scaled", "e", "g"))
    S, PR = o2["scores"], o2["probs"]

    def mixed(part, k):
        where = "at" if k < 4 else "sc" if k < 8 else "ssd"
        return o2[f"m{part}_{where}"][:, k - (0 if k < 4 else 4 if k < 8 else 8), :]

    BANK = ctx.enter_context(nc.psum_tensor("banks", [P, 8, SEQ], F32))

    def bank(i):
        return BANK[:, i, :]

    scratch = nc.dram_tensor("bias_rows", [HEADS, P, REL], F32).ap()

    layer_go = sem("layer_go")
    x_stored = sem("x_stored")
    con_landed, x_landed, setup_landed = sem("con_landed"), sem("x_landed"), sem("setup_landed")
    idr_done, eps_done = sem("idr_done"), sem("eps_done")
    bias_mm, bias_row, bias_stored = sem("bias_mm"), sem("bias_row"), sem("bias_stored")
    first_cleared = layer_end = sem("layer_end")
    par_landed = sem("par_landed")
    w_landed = [sem("w_landed0"), sem("w_landed1")]
    w_hi, w_lo = sem("w_hi"), sem("w_lo")
    w_used = sem("w_used")
    evac = [sem("evac0"), sem("evac1")]
    dve_step = sem("dve_step")
    sq_done, ss_done, ln_done, root_done = sem("sq_done"), sem("ss_done"), sem("ln_done"), sem("root_done")
    t_done = sem("t_done")
    n_hi, n_lo = sem("n_hi"), sem("n_lo")
    x_added = sem("x_added")
    tap_first, silu_done = sem("tap_first"), sem("silu_done")
    qk_sq, qk_ss, qk_ln, qk_root, qk_norm = (sem(n) for n in ("qk_sq", "qk_ss", "qk_ln", "qk_root", "qk_norm"))
    v_copied = sem("v_copied")
    cx_tap, sc_hi, sc_lo = sem("cx_tap"), sem("sc_hi_done"), sem("sc_lo_done")
    bias_landed = [sem("bias_landed0"), sem("bias_landed1")]
    at_qk, at_neg, at_exp, at_p = sem("at_qk"), sem("at_neg"), sem("at_exp"), sem("at_p")
    at_tr, at_ptc, at_pv, at_hi, at_lo = sem("at_tr"), sem("at_ptc"), sem("at_pv"), sem("at_hi"), sem("at_lo")
    dt_x, dt_e, dt_w, dt_ln, a_exp, dt_done, lndt_done, da_done = (
        sem(n) for n in ("dt_x", "dt_e", "dt_w", "dt_ln", "a_exp", "dt_done", "lndt_done", "da_done"))
    cs_mm, cs_row, cs_hi, cs_lo, cs_tr, cs_col = (sem(n) for n in ("cs_mm", "cs_row", "cs_hi_done", "cs_lo_done", "cs_tr", "cs_col"))
    dec_mm, dec_exp, ws_done = sem("dec_mm"), sem("dec_exp"), sem("ws_done")
    tok_tr, tok_copied = sem("tok_tr"), sem("tok_copied")
    cb_mm, cb_done, xs_done, st_mm, sin_done = (sem(n) for n in ("cb_mm", "cb_done", "xs_done", "st_mm", "sin_done"))
    ab_mm, seg_done, e_done, ea_done = (sem(n) for n in ("ab_mm", "seg_done", "e_done", "ea_done"))
    g_done, gs_done, y_mm, yo_mm, y_read, t_read, y_comb = (
        sem(n) for n in ("g_done", "gs_done", "y_mm", "yo_mm", "y_read", "t_read", "y_comb"))
    ff_tap, ff_silu, ff_hi, ff_lo = (sem(n) for n in ("ff_tap", "ff_silu_done", "ff_hi_done", "ff_lo_done"))
    last_cleared = ff_lo

    def par(col, n=1):
        return PAR[:, col:col + n] if isinstance(col, int) else PAR[:, bass.ds(col, n)]

    def tile_of(tensor, t):
        if isinstance(t, int):
            return tensor[:, t, :]
        return tensor[:, bass.ds(t, 1), :].rearrange("p a s -> p (a s)")

    def column(d, h):
        return d * DIR + h

    def direction_chunk(j):
        d, i = j % 2, j // 2
        return d, (i if d == 0 else QT - 1 - i)

    def rms_hi(name, k):
        if name in ("norm1", "norm2"):
            return HHI[:, k, :]
        return o2["mh_ssd"][:, 4 * int(name[-1]) + k, :]

    def rms_bank(name):
        return bank(7 if name == "ssd1" else 6)

    block = ctx.enter_context(nc.Block())

    @block.sync
    def _(sp):
        sp.dma_start(CON[:, :, :], a["constants"]).then_inc(con_landed, 16)
        sp.dma_start(X[:, :, :], a["x_t"].rearrange("(k p) s -> p k s", p=P)).then_inc(x_landed, 16)
        sp.dma_start(o2["onehot"][:, :], a["onehot"]).then_inc(setup_landed, 16)
        sp.dma_start(o2["log_count"][:, :], a["log_count"]).then_inc(setup_landed, 16)
        sp.dma_start(o2["table"][:, :], a["rel_table"]).then_inc(setup_landed, 16)

        def load(src, row, b, chunk, n=CHUNK, first=False):
            if not first:
                sp.wait_ge(w_lo, chunk - 1)
            sp.dma_start(W[:, b, 0:n], src[bass.ds(row, 1), :, 0:n].rearrange("a p n -> p (a n)"))\
                .then_inc(w_landed[b], 16)

        sp.sem_inc(layer_go, 1)
        with sp.Fori(0, DEPTH) as layer:
            sp.wait_ge(layer_go, layer + 1)
            sp.nop(nofuse=True)
            sp.dma_start(PAR[:, :], a["params"][bass.ds(layer, 1), :, :].rearrange("a p n -> p (a n)"))\
                .then_inc(par_landed, 16)
            for b in range(2):
                load(a["w_in"], layer * C_DT + b, b, b, first=True)
            with sp.Fori(0, C_DT // 2 - 1) as i:
                for b in range(2):
                    load(a["w_in"], layer * C_DT + (i * 2 + (2 + b)), b, i * 2 + (2 + b))
            for b in range(2):
                load(a["w_dt"], layer * 2 + b, b, C_DT + b, n=KT // 2 * 64)
            for b in range(2):
                load(a["w_out"], layer * (2 * KT) + b, b, C_OUT + b)
            sp.wait_ge(bias_stored, 16)
            for h in range(HEADS):
                if h < 2:
                    sp.wait_ge(w_used, C_OUT)
                else:
                    sp.wait_ge(at_neg, 4 * (h - 1))
                sp.dma_start(BIAS[:, h % 2, :], bass.AP(scratch.tensor, h * P * REL + P - 1, [[REL - 1, P], [1, TOEP]]))\
                    .then_inc(bias_landed[h % 2], 16)
            with sp.Fori(0, KT - 1) as i:
                for b in range(2):
                    load(a["w_out"], layer * (2 * KT) + (i * 2 + (2 + b)), b, i * 2 + (C_OUT + 2 + b))
            with sp.Fori(0, FF_T) as i:
                for b in range(2):
                    load(a["w_up"], layer * (2 * FF_T) + (i * 2 + b), b, i * 2 + (C_UP + b))
            with sp.Fori(0, KT // 2) as i:
                for j in range(2 * DOWN_C):
                    last = j % DOWN_C == DOWN_C - 1
                    load(a["w_down"], layer * (DOWN_C * KT) + (i * (2 * DOWN_C) + j), j % 2, i * (2 * DOWN_C) + (C_DOWN + j),
                         n=(FF_T - (DOWN_C - 1) * KT) * P if last else CHUNK)
            sp.wait_ge(layer_end, 4)
            sp.sem_clear(range(first_cleared.num, last_cleared.num + 1))
            sp.sem_inc(layer_go, 1)
        sp.dma_start(a["out_t"].rearrange("(k p) s -> p k s", p=P), X[:, :, :]).then_inc(x_stored, 16)
        sp.wait_ge(x_stored, 16)

    @block.gpsimd
    def _(pool):
        g = nc.gpsimd

        def w_low(b, done):
            pool.wait_ge(w_hi, done)
            g.tensor_tensor(WLO[:, b, :], W[:, b, :], WHI[:, b, :].bitcast(F32), ALU.subtract).then_inc(w_lo, 1)

        def low_next(first, count):
            with pool.Fori(0, count // 2) as i:
                for b in range(2):
                    w_low(b, i * 2 + (first + b + 3))

        def rms_low(name, dst):
            for k in range(RMS_TILES[name]):
                at = RMS_BASE[name] + k
                pool.wait_ge(n_hi, at + 1)
                g.tensor_tensor(dst(k), T[:, at % 2, :], rms_hi(name, k).bitcast(F32), ALU.subtract).then_inc(n_lo, 1)

        pool.wait_ge(bias_row, 2)
        g.dma_start(scratch, o2["bias_row"][:, :].unsqueeze(1).to_broadcast([HEADS, P, REL])).then_inc(bias_stored, 16)
        with pool.Fori(0, DEPTH) as layer:
            pool.wait_ge(layer_go, layer + 1)
            pool.nop(nofuse=True)
            pool.sem_inc(sc_lo, 1)
            pool.sem_inc(ff_lo, 1)
            w_low(0, 1)
            w_low(1, 2)
            rms_low("norm1", lambda k: HLO[:, k, :])
            low_next(0, C_SC)
            with pool.Fori(0, 2) as i:
                for j in range(6):
                    w_low(j % 2, i * 6 + (C_SC + j + 3))
                    if j % 3 == 2:
                        t = i * 2 + j // 3
                        pool.wait_ge(sc_hi, t + 2)
                        g.tensor_tensor(tile_of(o2["ml_sc"], t), SCP[:, :], tile_of(o2["mh_sc"], t).bitcast(F32),
                                        ALU.subtract).then_inc(sc_lo, 1)
            for b in range(2):
                w_low(b, C_DT + b + 3)

            pool.wait_ge(sc_lo, 5)
            def output(t):
                pool.wait_ge(y_read, t + 1)
                g.tensor_tensor(XC[:, t, 0:SEQ - P], XC[:, t, 0:SEQ - P], T[:, 1, 0:SEQ - P], ALU.add).then_inc(t_read, 1)
                pool.wait_ge(t_read, t + 1)
                g.tensor_tensor(Z[:, t, :], Z[:, t, :], XC[:, t, :], ALU.mult).then_inc(y_comb, 1)

            for grp in range(SSD_GROUPS):
                for j in range(6):
                    d, c = direction_chunk(j)
                    n, col = grp * 6 + j, column(d, 8 * grp)
                    pool.wait_ge(ws_done, 1)
                    pool.wait_ge(tok_copied, 8)
                    if n >= 2:
                        pool.wait_ge(st_mm, n - 1)
                    g.tensor_tensor(XS[:, j % 2, :].rearrange("p (h e) -> p h e", e=64),
                                    XT[:, c, 512 * grp:512 * grp + 512].rearrange("p (h e) -> p h e", e=64),
                                    WS[:, c, col:col + 8].unsqueeze(2).to_broadcast([P, 8, 64]), ALU.mult)\
                        .then_inc(xs_done, 1)
                for hh in range(8):
                    h = 8 * grp + hh
                    pool.wait_ge(g_done, h + 1)
                    if h >= 2:
                        pool.wait_ge(y_mm, h - 1)
                    g.tensor_tensor(G[:, h % 2, :], E[:, h % 2, 0, :], E[:, h % 2, 1, :], ALU.add).then_inc(gs_done, 1)
                    if hh % 2 == 0 and hh:
                        output(h // 2 - 1)
                output(4 * grp + 3)
            rms_low("ssd0", lambda k: o2["ml_ssd"][:, k, :])
            for b in range(2):
                w_low(b, C_OUT + b + 3)
            rms_low("ssd1", lambda k: o2["ml_ssd"][:, 4 + k, :])
            low_next(C_OUT + 2, 2 * KT - 2)
            rms_low("norm2", lambda k: HLO[:, k, :])
            with pool.Fori(0, FF_T // 2) as i:
                for j in range(4):
                    w_low(j % 2, i * 4 + (C_UP + j + 3))
                    if j % 2 == 1:
                        t = i * 2 + j // 2
                        pool.wait_ge(ff_hi, t + 2)
                        g.tensor_tensor(tile_of(FLO, t), FP[:, :], tile_of(FHI, t).bitcast(F32), ALU.subtract)\
                            .then_inc(ff_lo, 1)
            low_next(C_DOWN, DOWN_C * KT - 2)
            pool.drain().then_inc(layer_end, 1)

    @block.scalar
    def _(act):
        sc = nc.scalar

        def w_high(b, landed):
            act.wait_ge(w_landed[b], landed)
            sc.activation(WHI[:, b, :], W[:, b, :], ACT.Copy).then_inc(w_hi, 1)

        def high_next(c, i=0, step=0):
            act.wait_ge(w_used, i * step + (c + 1))
            w_high(c % 2, i * (8 * step) + 16 * (c // 2 + 2))

        def rms_square(name, k, src):
            at = RMS_BASE[name] + k
            if at >= 2:
                act.wait_ge(ss_done, at - 1)
            sc.activation(SQ[:, at % 2, :], src, ACT.Square).then_inc(sq_done, 1)

        def rms_root(name, mean_scale):
            act.wait_ge(ss_done, RMS_BASE[name] + RMS_TILES[name])
            sc.activation(RSTD[:, :], rms_bank(name), ACT.Ln, bias=EPSC[:, 0:1], scale=mean_scale).then_inc(ln_done, 1)
            act.wait_ge(ln_done, list(RMS_BASE).index(name) + 1)
            sc.activation(RSTD[:, :], RSTD[:, :], ACT.Exp, scale=-0.5).then_inc(root_done, 1)

        def rms_high(name):
            for k in range(RMS_TILES[name]):
                act.wait_ge(t_done, RMS_BASE[name] + k + 1)
                sc.activation(rms_hi(name, k), T[:, k % 2, :], ACT.Copy).then_inc(n_hi, 1)

        act.wait_ge(con_landed, 16)
        sc.activation(IDR[:, :], con["ident"], ACT.Copy).then_inc(idr_done, 1)
        act.wait_ge(eps_done, 2)
        act.wait_ge(x_landed, 16)
        with act.Fori(0, DEPTH) as layer:
            act.wait_ge(layer_go, layer + 1)
            act.nop(nofuse=True)
            act.wait_ge(par_landed, 16)
            w_high(0, 16)
            for k in range(KT):
                rms_square("norm1", k, X[:, k, :])
            w_high(1, 16)
            rms_root("norm1", 1.0 / D_MODEL)
            rms_high("norm1")

            def centre_tap(b, tile, acc_read=None):
                if acc_read is not None:
                    act.wait_ge(silu_done, acc_read)
                col = tile * 8 + PA_CONV7
                sc.activation(ACC7[:, b, :], bank(b), ACT.Identity, bias=par(col + 7), scale=par(col + 3)).then_inc(tap_first, 1)

            def silu(b, dst, done):
                act.wait_ge(evac[b], done)
                sc.activation(dst, ACC7[:, b, :], ACT.Silu).then_inc(silu_done, 1)

            high_next(0)
            centre_tap(0, 0)
            high_next(1)
            centre_tap(1, 1)
            silu(0, XC[:, 0, :], 1)
            with act.Fori(0, 3) as i:
                for b in range(2):
                    high_next(2 + b, i, 2)
                    centre_tap(b, i * 2 + (2 + b), i * 2 + (1 + b))
                    silu(1 - b, tile_of(XC, i * 2 + (1 + b)), i + (1 + b))
            for n in range(8, 12):
                high_next(n)
                centre_tap(n % 2, n, n - 1)
                silu((n - 1) % 2, XC[:, 7, :] if n == 8 else BC[:, n - 9, :], (n - 1) // 2 + 1)
            silu(1, BC[:, 3, :], 6)

            for dst, c in ((Q, C_QK), (K, C_QK + 4)):
                with act.Fori(0, 2) as i:
                    for b in range(2):
                        high_next(c + b, i, 2)
                        sc.activation(tile_of(dst, i * 2 + b), bank(b), ACT.Copy).then_inc(evac[b], 1)
            for j in range(4):
                high_next(C_V + j)
            for c in range(QT):
                sc.activation(V[:, c, :], bank(2 + c), ACT.Copy).then_inc(v_copied, 1)
            for n in range(8):
                act.wait_ge(qk_ss, n + 1)
                sc.activation(QKSQ[:, n, :], bank(6 + n % 2), ACT.Ln, bias=EPSC[:, 1 - n // 4:2 - n // 4],
                              scale=1.0 if n < 4 else 1.0 / HEAD_DIM).then_inc(qk_ln, 1)
            act.wait_ge(qk_ln, 8)
            sc.activation(QKSQ[:, :, :], QKSQ[:, :, :], ACT.Exp, scale=-0.5).then_inc(qk_root, 1)
            with act.Fori(0, 4) as i:
                for b in range(2):
                    high_next(C_Z + b, i, 2)
                    sc.activation(tile_of(Z, i * 2 + b), bank(b), ACT.Silu).then_inc(evac[b], 1)
            act.wait_ge(bias_stored, 16)
            with act.Fori(0, 2) as i:
                for j in range(6):
                    t = i * 2 + j // 3
                    high_next(C_SC + j, i, 6)
                    if j % 3 == 0:
                        act.wait_ge(evac[j % 2], i * 3 + (N_SC + j - 2) // 2 + 1)
                        sc.activation(SCC[:, :], bank(j % 2), ACT.Copy).then_inc(evac[j % 2], 1)
                    if j % 3 == 1:
                        act.wait_ge(evac[j % 2], i * 3 + ((N_SC + j) // 2 + 1))
                        act.wait_ge(sc_hi, t + 1)
                        sc.activation(SCA[:, :], CX[:, :], ACT.Identity, bias=par(t * 4 + (PA_SC + 3)),
                                      scale=par(t * 4 + (PA_SC + 1))).then_inc(cx_tap, 1)
            for b in range(2):
                high_next(C_DT + b)

            act.wait_ge(dt_x, 1)
            sc.activation(SM[:, 1, :], SM[:, 1, :], ACT.Exp).then_inc(dt_e, 1)
            sc.activation(par(PA_ALOG, 64), par(PA_ALOG, 64), ACT.Exp).then_inc(a_exp, 1)
            act.wait_ge(dt_w, 1)
            sc.activation(SM[:, 3, :], SM[:, 2, :], ACT.Ln).then_inc(dt_ln, 1)
            act.wait_ge(dt_done, 1)
            sc.activation(SM[:, 2, :], SM[:, 2, :], ACT.Ln).then_inc(lndt_done, 1)

            def at_evac(u):
                h, qt = u // 4, u % 4
                act.wait_ge(at_tr, u + 1)
                if h >= 2:
                    act.wait_ge(at_pv, h - 1)
                sc.activation(PTS[:, h % 2, :, qt * P:qt * P + P], bank(4 + u % 2).rearrange("p (j i) -> p j i", i=P),
                              ACT.Copy).then_inc(at_ptc, 1)

            def at_out(t):
                act.wait_ge(at_pv, 2 * t + 2)
                sc.activation(o2["mh_at"][:, t, :], bank(6 + t % 2), ACT.Copy).then_inc(at_hi, 1)

            for u in range(4 * HEADS):
                act.wait_ge(at_neg, u + 1)
                if u >= 2:
                    act.wait_ge(at_tr, u - 1)
                sc.activation(PR[:, u % 2, :], S[:, u % 2, :], ACT.Exp, bias=NEGMAX[:, u % 4:u % 4 + 1], scale=-1.0,
                              accum_out=DEN[:, u % 4:u % 4 + 1]).then_inc(at_exp, 1)
                if u >= 1:
                    at_evac(u - 1)
                if u % 8 == 3 and u > 8:
                    at_out(u // 8 - 1)
            at_evac(4 * HEADS - 1)
            at_out(HEADS // 2 - 1)

            act.wait_ge(cs_mm, 1)
            sc.activation(T[0:64, 0, :], BANK[0:64, 2, :], ACT.Copy).then_inc(cs_row, 1)
            sc.activation(CSHI[0:64, :], BANK[0:64, 2, :], ACT.Copy).then_inc(cs_hi, 1)
            act.wait_ge(dec_mm, 1)
            sc.activation(EW[:, :, :], bank(4).rearrange("p (c n) -> p c n", n=P), ACT.Exp).then_inc(dec_exp, 1)
            for n in range(10):
                act.wait_ge(tok_tr, n + 1)
                if n < 8:
                    dst, src = XT[:, n // 2, (n % 2) * 512:(n % 2) * 512 + 512], bank(5 + n % 2)
                else:
                    dst, src = BT[:, 2 * (n - 8):2 * (n - 8) + 2, :], bank(5 + n % 2).rearrange("p (c n) -> p c n", n=256)
                sc.activation(dst, src, ACT.Copy).then_inc(tok_copied, 1)
            for h in range(SSD_HEADS):
                half = slice(64 * (h % 2), 64 * (h % 2) + 64)
                act.wait_ge(seg_done, h + 1)
                sc.activation(E[:, h % 2, :, :], E[:, h % 2, :, :], ACT.Exp).then_inc(e_done, 1)
                if h >= 4:
                    act.wait_ge(y_read, h // 2 - 1)
                sc.activation(EA[half, (h // 2) % 2, :, :], BANK[half, 2 + 2 * (h % 2):4 + 2 * (h % 2), :], ACT.Exp)\
                    .then_inc(ea_done, 1)
            for t in range(8):
                act.wait_ge(y_comb, t + 1)
                rms_square(f"ssd{t // 4}", t % 4, Z[:, t, :])
            rms_root("ssd0", 1.0 * SSD_GROUPS / SSD_W)
            rms_high("ssd0")
            high_next(C_OUT)
            high_next(C_OUT + 1)
            rms_root("ssd1", 1.0 * SSD_GROUPS / SSD_W)
            rms_high("ssd1")

            for n in range(2, 2 * KT):
                high_next(C_OUT + n)
                if n in OUT_ENDS:
                    act.wait_ge(x_added, OUT_ENDS[n] + 1)
                    rms_square("norm2", OUT_ENDS[n], X[:, OUT_ENDS[n], :])
            rms_root("norm2", 1.0 / D_MODEL)
            rms_high("norm2")

            with act.Fori(0, FF_T // 2) as i:
                for j in range(4):
                    pb, t, col = j // 2, i * 2 + j // 2, i * 16 + (PA_FF + 4 * j)
                    high_next(C_UP + j, i, 4)
                    sc.activation((FG, FV)[j % 2][:, pb, :], bank(j % 2), ACT.Identity, bias=par(col + 3), scale=par(col + 1))\
                        .then_inc(ff_tap, 1)
                    if j % 2 == 1:
                        act.wait_ge(evac[0], t + (N_UP // 2 + 1))
                        act.wait_ge(ff_hi, t + 1)
                        sc.activation(FS[:, :], FG[:, pb, :], ACT.Silu).then_inc(ff_silu, 1)
            with act.Fori(0, (DOWN_C * KT - 2) // 2) as i:
                for b in range(2):
                    high_next(C_DOWN + b, i, 2)
            act.drain().then_inc(layer_end, 1)

    @block.vector
    def _(dve):
        v = nc.vector
        v.memset(EPSC[:, 0:1], EPS).then_inc(eps_done, 1)
        v.memset(EPSC[:, 1:2], EPS * HEAD_DIM).then_inc(eps_done, 1)
        dve.wait_ge(setup_landed, 48)
        for r in range(2):
            dve.wait_ge(bias_mm, r + 1)
            v.tensor_tensor(o2["bias_row"][:, 512 * r:512 * r + 512], BANK[0:HEADS, r, :],
                            o2["log_count"][:, 512 * r:512 * r + 512], ALU.add).then_inc(bias_row, 1)
        dve.wait_ge(x_landed, 16)
        dve.wait_ge(con_landed, 16)
        with dve.Fori(0, DEPTH) as layer:
            dve.wait_ge(layer_go, layer + 1)
            dve.nop(nofuse=True)
            dve.sem_inc(sc_hi, 1)
            dve.sem_inc(ff_hi, 1)
            dve.wait_ge(par_landed, 16)
            step = Steps(dve, dve_step)

            def rms(name, src, gain):
                base = RMS_BASE[name]
                dve.wait_ge(root_done, list(RMS_BASE).index(name) + 1)
                for k in range(RMS_TILES[name]):
                    if base + k >= 2:
                        dve.wait_ge(n_lo, base + k - 1)
                    v.scalar_tensor_tensor(T[:, k % 2, :], src(k), par(gain + k), RSTD[:, :], ALU.mult, ALU.mult)\
                        .then_inc(t_done, 1)

            def taps(acc, src, col, offsets, last=None):
                for m, (tap, o) in enumerate(offsets):
                    lo, hi = max(0, -o), SEQ - max(0, o)
                    ins = v.scalar_tensor_tensor(acc[:, lo:hi], src[:, lo + o:hi + o], par(col + tap), acc[:, lo:hi],
                                                 ALU.mult, ALU.add)
                    if last is not None and m == len(offsets) - 1:
                        ins.then_inc(last, 1)
                    else:
                        step(ins)

            rms("norm1", lambda k: X[:, k, :], PA_N1)
            seven = [(tap, tap - SSD_TAPS // 2) for tap in range(SSD_TAPS) if tap != SSD_TAPS // 2]
            with dve.Fori(0, 6) as i:
                step.enter(i, 10)
                for b in range(2):
                    dve.wait_ge(tap_first, i * 2 + (b + 1))
                    taps(ACC7[:, b, :], bank(b), i * 16 + (PA_CONV7 + 8 * b), seven, last=evac[b])
                step.leave(6)
            for n in range(8):
                dve.wait_ge(evac[n % 2], (N_QK + n) // 2 + 1)
                src = tile_of((Q, K)[n // 4], n % 4)
                v.tensor_tensor(QKSQ[:, n, :], src, src, ALU.mult).then_inc(qk_sq, 1)
            for n in range(8):
                dve.wait_ge(qk_root, 1)
                src = tile_of((Q, K)[n // 4], n % 4)
                v.scalar_tensor_tensor(src, src, par((PA_QG, PA_KG)[n // 4]), QKSQ[:, n, :], ALU.mult, ALU.mult)\
                    .then_inc(qk_norm, 1)
            with dve.Fori(0, 2) as i:
                step.enter(i, 4)
                for j in range(6):
                    b, t = j % 2, i * 2 + j // 3
                    if j % 3 == 1:
                        dve.wait_ge(w_used, i * 6 + (C_SC + j + 1))
                        dve.wait_ge(evac[1 - b], i * 3 + ((N_SC + j - 1) // 2 + 1))
                        v.tensor_tensor(CX[:, :], bank(b), SCC[:, :], ALU.mult).then_inc(evac[b], 1)
                        dve.wait_ge(cx_tap, t + 1)
                        taps(SCA, CX, t * 4 + PA_SC, [(0, -1), (2, 1)])
                    if j % 3 == 2:
                        dve.wait_ge(w_used, i * 6 + (C_SC + j + 1))
                        dve.wait_ge(sc_lo, t + 1)
                        v.tensor_tensor(SCP[:, :], bank(b), SCA[:, :], ALU.mult).then_inc(evac[b], 1)
                        dve.wait_ge(evac[b], i * 3 + ((N_SC + j) // 2 + 1))
                        v.tensor_copy(tile_of(o2["mh_sc"], t), SCP[:, :]).then_inc(sc_hi, 1)
                step.leave(2)

            dve.wait_ge(w_used, C_OUT)
            for c in range(QT):
                step(v.tensor_tensor(SM[:, 0, 64 * c:64 * c + 64], BANK[:, 2 + c, 0:64], par(PA_DTB, 64), ALU.add))
            dtf = DT[:, :, :].rearrange("p c n -> p (c n)")
            daf = DA[:, :, :].rearrange("p c n -> p (c n)")
            step(v.tensor_scalar(dtf, SM[:, 0, :], 0.0, None, ALU.max))
            step(v.tensor_scalar(SM[:, 1, :], SM[:, 0, :], 0.0, None, ALU.min))
            v.tensor_tensor(SM[:, 1, :], SM[:, 1, :], dtf, ALU.subtract).then_inc(dt_x, 1)
            dve.wait_ge(dt_e, 1)
            v.tensor_scalar(SM[:, 2, :], SM[:, 1, :], 1.0, None, ALU.add).then_inc(dt_w, 1)
            dve.wait_ge(dt_w, 1)
            step(v.tensor_scalar(SM[:, 0, :], SM[:, 2, :], 1.0, None, ALU.subtract))
            step(v.tensor_scalar(daf, SM[:, 0, :], 0.0, None, ALU.is_equal))
            step(v.tensor_tensor(SM[:, 0, :], SM[:, 0, :], daf, ALU.add))
            step(v.reciprocal(SM[:, 0, :], SM[:, 0, :]))
            dve.wait_ge(dt_ln, 1)
            step(v.tensor_tensor(SM[:, 3, :], SM[:, 3, :], daf, ALU.add))
            step(v.tensor_tensor(SM[:, 3, :], SM[:, 3, :], SM[:, 0, :], ALU.mult))
            step(v.tensor_tensor(SM[:, 3, :], SM[:, 3, :], SM[:, 1, :], ALU.mult))
            step(v.tensor_tensor(dtf, dtf, SM[:, 3, :], ALU.add))
            v.tensor_scalar(SM[:, 2, :], dtf, 1e-37, None, ALU.max).then_inc(dt_done, 1)
            dve.wait_ge(a_exp, 1)
            v.scalar_tensor_tensor(DA[:, :, :], DT[:, :, :], -1.0, par(PA_ALOG, 64).unsqueeze(1).to_broadcast([P, QT, 64]),
                                   ALU.mult, ALU.mult).then_inc(da_done, 1)

            def at_neg_max(u):
                h, qt = u // 4, u % 4
                dve.wait_ge(at_qk, u + 1)
                dve.wait_ge(bias_landed[h % 2], 16 * (h // 2 + 1))
                if u >= 2:
                    dve.wait_ge(at_exp, u - 1)
                at = SEQ - P - P * qt
                v.tensor_tensor_reduce(S[:, u % 2, :], bank(2 + u % 2), BIAS[:, h % 2, at:at + SEQ], scale=-1.0, scalar=3e38,
                                       op0=ALU.add, op1=ALU.min, accum_out=NEGMAX[:, u % 4:u % 4 + 1]).then_inc(at_neg, 1)

            def at_normalize(u):
                dve.wait_ge(at_exp, u + 1)
                col = slice(u % 4, u % 4 + 1)
                step(v.reciprocal(RDEN[:, col], DEN[:, col]))
                v.tensor_scalar(PR[:, u % 2, :], PR[:, u % 2, :], RDEN[:, col], None, ALU.mult).then_inc(at_p, 1)

            def at_low(t):
                dve.wait_ge(at_hi, t + 1)
                v.tensor_tensor(o2["ml_at"][:, t, :], bank(6 + t % 2), o2["mh_at"][:, t, :].bitcast(F32), ALU.subtract)\
                    .then_inc(at_lo, 1)

            at_neg_max(0)
            for u in range(4 * HEADS):
                if u + 1 < 4 * HEADS:
                    at_neg_max(u + 1)
                at_normalize(u)
                if u % 8 == 4 and u > 8:
                    at_low(u // 8 - 1)
            at_low(HEADS // 2 - 1)

            dve.wait_ge(cs_hi, 1)
            v.tensor_tensor(CSLO[0:64, :], BANK[0:64, 2, :], CSHI[0:64, :].bitcast(F32), ALU.subtract).then_inc(cs_lo, 1)
            dve.wait_ge(dec_exp, 1)
            v.tensor_tensor(WS[:, :, :], EW[:, :, 0:64], DT[:, :, :], ALU.mult).then_inc(ws_done, 1)
            dve.wait_ge(cs_tr, 1)
            dve.wait_ge(lndt_done, 1)
            v.tensor_tensor(AS[:, :, :].rearrange("p c n -> p (c n)"), BANK[:, 3, 0:256], SM[:, 2, :], ALU.subtract)\
                .then_inc(cs_col, 1)
            dve.wait_ge(cs_col, 1)

            def chunks(x):
                return x.rearrange("p (c l) -> p c l", l=P)

            def seg(h):
                dve.wait_ge(ab_mm, h + 1)
                if h >= 2:
                    dve.wait_ge(gs_done, h - 1)
                columns = AS[:, :, h:h + DIR + 1:DIR].rearrange("p c d -> p d c").unsqueeze(3).to_broadcast([P, 2, QT, P])
                step(v.tensor_tensor(E[:, h % 2, :, :].rearrange("p d (c l) -> p d c l", l=P),
                                     BANK[:, 2 + 2 * (h % 2):4 + 2 * (h % 2), :].rearrange("p d (c l) -> p d c l", l=P),
                                     columns, ALU.subtract))
                v.tensor_scalar(E[:, h % 2, :, :], E[:, h % 2, :, :], 80.0, None, ALU.min).then_inc(seg_done, 1)

            def weigh(h):
                dve.wait_ge(e_done, h + 1)
                v.tensor_tensor(E[:, h % 2, :, :], E[:, h % 2, :, :], CB[:, :, :], ALU.mult).then_inc(g_done, 1)

            def combine(t):
                dve.wait_ge(y_mm, 2 * t + 2)
                step(v.scalar_tensor_tensor(XC[:, t, :], XC[:, t, :], par(PA_D + t), bank(6 + t % 2), ALU.mult, ALU.add))
                dve.wait_ge(yo_mm, t + 1)
                dve.wait_ge(ea_done, 2 * t + 2)
                spans = (slice(P, SEQ), slice(0, SEQ - P))
                if t:
                    dve.wait_ge(t_read, t)
                for d in range(2):
                    step(v.tensor_tensor(T[:, d, spans[d]], BANK[:, d, spans[d]], EA[:, t % 2, d, spans[d]], ALU.mult))
                v.tensor_tensor(XC[:, t, spans[0]], XC[:, t, spans[0]], T[:, 0, spans[0]], ALU.add).then_inc(y_read, 1)

            for grp in range(SSD_GROUPS):
                dve.wait_ge(cb_mm, grp + 1)
                for d in range(2):
                    v.tensor_tensor(chunks(CB[:, d, :]), chunks(bank(6)),
                                    con[("le", "ge")[d]].unsqueeze(1).to_broadcast([P, QT, P]), ALU.mult).then_inc(cb_done, 1)
                dve.wait_ge(cb_done, 2 * grp + 2)
                for j in range(6):
                    (d, c), i, n = direction_chunk(j), j // 2, 6 * grp + j
                    if i == 0:
                        dve.wait_ge(st_mm, n + 1)
                        v.tensor_copy(SIN[:, d, 0, :], bank(j % 2)).then_inc(sin_done, 1)
                        continue
                    if grp:
                        dve.wait_ge(y_read, 4)
                        dve.wait_ge(t_read, 4)
                    col = 64 + column(d, 8 * grp)
                    dve.wait_ge(sin_done, n - 1)
                    step(v.tensor_tensor(T[:, d, :].rearrange("p (h e) -> p h e", e=64),
                                         SIN[:, d, i - 1, :].rearrange("p (h e) -> p h e", e=64),
                                         EW[:, c, col:col + 8].unsqueeze(2).to_broadcast([P, 8, 64]), ALU.mult))
                    dve.wait_ge(st_mm, n + 1)
                    v.tensor_tensor(SIN[:, d, i, :], bank(j % 2), T[:, d, :], ALU.add).then_inc(sin_done, 1)
                h0 = 8 * grp
                seg(h0)
                for hh in range(8):
                    if hh < 7:
                        seg(h0 + hh + 1)
                    weigh(h0 + hh)
                    if hh % 2 == 0 and hh:
                        combine((h0 + hh) // 2 - 1)
                combine(4 * grp + 3)
            dve.wait_ge(t_read, 8)
            for grp in range(SSD_GROUPS):
                rms(f"ssd{grp}", lambda k: Z[:, 4 * grp + k, :], PA_SNG + 4 * grp)

            for m in range(KT):
                dve.wait_ge(w_used, C_OUT + OUT_ORDER.index((m, 1)) + 1)
                v.tensor_tensor(X[:, m, :], bank(m % 6), X[:, m, :], ALU.add).then_inc(x_added, 1)
            rms("norm2", lambda k: X[:, k, :], PA_N2)
            with dve.Fori(0, FF_T // 2) as i:
                step.enter(i, 6)
                for j in range(4):
                    b, pb, t = j % 2, j // 2, i * 2 + j // 2
                    dve.wait_ge(ff_tap, i * 4 + (j + 1))
                    taps((FG, FV)[b][:, pb, :], bank(b), i * 16 + (PA_FF + 4 * j), [(0, -1), (2, 1)], last=evac[b])
                    if b == 1:
                        dve.wait_ge(evac[b], t + (N_UP // 2 + 1))
                        dve.wait_ge(ff_silu, t + 1)
                        dve.wait_ge(ff_lo, t + 1)
                        step(v.tensor_tensor(FP[:, :], FS[:, :], FV[:, pb, :], ALU.mult))
                        v.tensor_copy(tile_of(FHI, t), FP[:, :]).then_inc(ff_hi, 1)
                step.leave(FF_T // 2)
            with dve.Fori(0, KT // 2) as i:
                for b in range(2):
                    dve.wait_ge(w_used, i * (2 * DOWN_C) + (C_DOWN + DOWN_C * (b + 1)))
                    v.tensor_tensor(tile_of(X, i * 2 + b), bank(b), tile_of(X, i * 2 + b), ALU.add).then_inc(evac[b], 1)
            dve.drain().then_inc(layer_end, 1)

    @block.tensor
    def _(pe):
        mm, transpose = nc.tensor.matmul, nc.tensor.transpose

        pe.wait_ge(setup_landed, 48)
        for r in range(2):
            mm(BANK[0:HEADS, r, :], o2["table"][:, :], o2["onehot"][:, 512 * r:512 * r + 512], start=True, stop=True)\
                .then_inc(bias_mm, 1)
        pe.wait_ge(con_landed, 16)
        pe.wait_ge(idr_done, 1)

        def products(out, blocks, start, stop):
            for k, (whi, wlo, hhi, hlo) in enumerate(blocks):
                for p, (l, r) in enumerate(((whi, hhi), (whi, hlo), (wlo, hhi))):
                    ins = mm(out, l, r, start=start and k == 0 and p == 0, stop=stop and k == len(blocks) - 1 and p == 2)
            return ins

        def chunk_blocks(b, hs, n=KT):
            at = [slice(P * k, P * k + P) for k in range(n)]
            return [(WHI[:, b, at[k]], WLO[:, b, at[k]], *hs(k)) for k in range(n)]

        def normed(k):
            return HHI[:, k, :], HLO[:, k, :]

        def first_tile(chunk, base):
            pe.wait_ge(w_lo, chunk + 1)
            for k, block in enumerate(chunk_blocks(0, normed)):
                pe.wait_ge(n_lo, base + k + 1)
                ins = products(bank(0), [block], k == 0, k == KT - 1)
            ins.then_inc(w_used, 1)

        def tiles(c0, n0, count):
            with pe.Fori(0, count // 2) as i:
                for b in range(2):
                    pe.wait_ge(w_lo, i * 2 + (c0 + b + 1))
                    if n0:
                        pe.wait_ge(evac[b], i + n0 // 2)
                    products(bank(b), chunk_blocks(b, normed), True, True).then_inc(w_used, 1)

        def rms_sum(name, k):
            pe.wait_ge(sq_done, RMS_BASE[name] + k + 1)
            mm(rms_bank(name), con["ones"], SQ[:, k % 2, :], start=k == 0, stop=k == RMS_TILES[name] - 1).then_inc(ss_done, 1)

        with pe.Fori(0, DEPTH) as layer:
            pe.wait_ge(layer_go, layer + 1)
            pe.nop(nofuse=True)
            for k in range(KT):
                rms_sum("norm1", k)
            first_tile(0, RMS_BASE["norm1"])
            pe.wait_ge(w_lo, 2)
            products(bank(1), chunk_blocks(1, normed), True, True).then_inc(w_used, 1)
            tiles(2, 2, C_QK - 2)
            tiles(C_QK, N_QK, 8)
            for j in range(4):
                pe.wait_ge(w_lo, C_V + j + 1)
                for c in range(QT):
                    at = slice(P * c, P * c + P)
                    blocks = [(HHI[:, 2 * j + k, at], HLO[:, 2 * j + k, at], WHI[:, j % 2, 512 * k:512 * k + 512],
                               WLO[:, j % 2, 512 * k:512 * k + 512]) for k in range(2)]
                    ins = products(bank(2 + c), blocks, j == 0, j == 3)
                ins.then_inc(w_used, 1)
            for n in range(8):
                pe.wait_ge(qk_sq, n + 1)
                if n >= 2:
                    pe.wait_ge(qk_ln, n - 1)
                mm(bank(6 + n % 2), con["headones"], QKSQ[:, n, :], start=True, stop=True).then_inc(qk_ss, 1)
            tiles(C_Z, N_Z, 8)
            tiles(C_SC, N_SC, 12)
            pe.wait_ge(v_copied, QT)
            for j in range(2):
                pe.wait_ge(w_lo, C_DT + j + 1)
                for c in range(QT):
                    at = slice(P * c, P * c + P)
                    blocks = [(HHI[:, 4 * j + k, at], HLO[:, 4 * j + k, at], WHI[:, j, 64 * k:64 * k + 64],
                               WLO[:, j, 64 * k:64 * k + 64]) for k in range(4)]
                    ins = products(BANK[:, 2 + c, 0:64], blocks, j == 0, j == 1)
                ins.then_inc(w_used, 1)

            def qk(u):
                h, qt = u // 4, u % 4
                hs = slice(64 * (h % 2), 64 * (h % 2) + 64)
                if u >= 2:
                    pe.wait_ge(at_neg, u - 1)
                mm(bank(2 + u % 2), Q[hs, h // 2, P * qt:P * qt + P], K[hs, h // 2, :], start=True, stop=True)\
                    .then_inc(at_qk, 1)

            def turn(u):
                pe.wait_ge(at_p, u + 1)
                if u >= 2:
                    pe.wait_ge(at_ptc, u - 1)
                for j in range(QT):
                    ins = transpose(BANK[:, 4 + u % 2, P * j:P * j + P], PR[:, u % 2, P * j:P * j + P], con["ident"])
                ins.then_inc(at_tr, 1)

            def pv(h):
                t, half = h // 2, 64 * (h % 2)
                pe.wait_ge(at_ptc, 4 * h + 4)
                if t >= 2:
                    pe.wait_ge(at_lo, t - 1)
                for j in range(QT):
                    ins = mm(BANK[half:half + 64, 6 + t % 2, :], V[:, j, 64 * h:64 * h + 64], PTS[:, h % 2, j, :],
                             start=j == 0, stop=j == QT - 1)
                ins.then_inc(at_pv, 1)

            pe.wait_ge(qk_norm, 8)
            pe.wait_ge(dt_x, 1)
            qk(0)
            qk(1)
            for u in range(4 * HEADS):
                if u + 2 < 4 * HEADS:
                    qk(u + 2)
                turn(u)
                if u % 4 == 1 and u > 4:
                    pv(u // 4 - 1)
            pv(HEADS - 1)

            pe.wait_ge(da_done, 1)
            pe.wait_ge(at_lo, HEADS // 2)
            for c in range(QT):
                for d in range(2):
                    ins = mm(BANK[DIR * d:DIR * d + DIR, 2, P * c:P * c + P], DA[:, c, DIR * d:DIR * d + DIR],
                             con[("le", "ge")[d]], start=True, stop=True)
            ins.then_inc(cs_mm, 1)
            for c in range(QT):
                for d in range(2):
                    mm(BANK[:, 4, P * c + DIR * d:P * c + DIR * d + DIR], con[("gt", "lt")[d]],
                       DA[:, c, DIR * d:DIR * d + DIR], start=True, stop=True)
                ins = mm(BANK[:, 4, P * c + 64:P * c + P], con["ones"], DA[:, c, :], start=True, stop=True)
            ins.then_inc(dec_mm, 1)
            pe.wait_ge(cs_row, 1)
            for c in range(QT):
                ins = transpose(BANK[:, 3, 64 * c:64 * c + 64], T[0:64, 0, P * c:P * c + P], con["ident"][0:64, 0:64])
            ins.then_inc(cs_tr, 1)
            for n in range(10):
                if n >= 2:
                    pe.wait_ge(tok_copied, n - 1)
                for m in range(4):
                    if n < 8:
                        src = XC[:, 4 * (n % 2) + m, P * (n // 2):P * (n // 2) + P]
                    else:
                        c = 2 * (n - 8) + m // 2
                        src = BC[:, m % 2, P * c:P * c + P]
                    ins = transpose(BANK[:, 5 + n % 2, P * m:P * m + P], src, con["ident"])
                ins.then_inc(tok_tr, 1)

            def row_sums(h):
                if h >= 2:
                    pe.wait_ge(ea_done, h - 1)
                for d in range(2):
                    row = IDR[0:64, column(d, h):column(d, h) + 1].to_broadcast([64, P])
                    mm(bank(2 + 2 * (h % 2) + d), row, CSHI[0:64, :], start=True, stop=False)
                    ins = mm(bank(2 + 2 * (h % 2) + d), row, CSLO[0:64, :], start=False, stop=True)
                ins.then_inc(ab_mm, 1)

            def within(h):
                t, half, grp = h // 2, 64 * (h % 2), h // 8
                pe.wait_ge(gs_done, h + 1)
                if t >= 2:
                    pe.wait_ge(y_read, t - 1)
                for c in range(QT):
                    ins = mm(BANK[half:half + 64, 6 + t % 2, P * c:P * c + P], XT[:, c, 64 * h:64 * h + 64],
                             G[:, h % 2, P * c:P * c + P], start=True, stop=True)
                ins.then_inc(y_mm, 1)

            def from_states(t):
                grp, at = t // 4, slice(P * (t % 4), P * (t % 4) + P)
                pe.wait_ge(y_read, t) if t else None
                for i in range(QT - 1):
                    for d in range(2):
                        c = i + 1 if d == 0 else QT - 2 - i
                        ins = mm(BANK[:, d, P * c:P * c + P], SIN[:, d, i, at], BC[:, 2 + grp, P * c:P * c + P],
                                 start=True, stop=True)
                ins.then_inc(yo_mm, 1)

            pe.wait_ge(cs_lo, 1)
            pe.wait_ge(cs_col, 1)
            pe.wait_ge(dec_exp, 1)
            for grp in range(SSD_GROUPS):
                pe.wait_ge(tok_copied, 10)
                if grp:
                    pe.wait_ge(y_read, 4 * grp)
                for c in range(QT):
                    at = slice(P * c, P * c + P)
                    ins = mm(BANK[:, 6, at], BC[:, grp, at], BC[:, 2 + grp, at], start=True, stop=True)
                ins.then_inc(cb_mm, 1)
                for j in range(6):
                    d, c = direction_chunk(j)
                    n = 6 * grp + j
                    pe.wait_ge(xs_done, n + 1)
                    if j >= 2:
                        pe.wait_ge(sin_done, n - 1)
                    mm(bank(j % 2), BT[:, c, P * grp:P * grp + P], XS[:, j % 2, :], start=True, stop=True).then_inc(st_mm, 1)
                pe.wait_ge(cb_done, 2 * grp + 2)
                pe.wait_ge(sin_done, 6 * grp + 6)
                row_sums(8 * grp)
                row_sums(8 * grp + 1)
                for hh in range(8):
                    h = 8 * grp + hh
                    if hh % 2 == 0:
                        from_states(h // 2)
                    if hh < 6:
                        row_sums(h + 2)
                    within(h)

            def out_products(n):
                m, j = OUT_ORDER[n]
                pe.wait_ge(w_lo, C_OUT + n + 1)
                if m >= 6:
                    pe.wait_ge(x_added, m - 5)
                products(bank(m % 6), chunk_blocks(n % 2, lambda k: (mixed("h", 8 * j + k), mixed("l", 8 * j + k))),
                         j == 0, j == 1).then_inc(w_used, 1)

            pe.wait_ge(sc_lo, 5)
            pe.wait_ge(at_lo, 4)
            pe.wait_ge(y_read, 8)
            pe.wait_ge(ea_done, SSD_HEADS)
            out_products(0)
            for t in range(8):
                rms_sum(f"ssd{t // 4}", t % 4)
            for n in range(1, 2 * KT):
                if n == 6:
                    pe.wait_ge(n_lo, RMS_BASE["norm2"])
                out_products(n)
                if n - 1 in OUT_ENDS:
                    if OUT_ENDS[n - 1] == 0:
                        pe.wait_ge(ln_done, 2 + 1)
                    rms_sum("norm2", OUT_ENDS[n - 1])
            rms_sum("norm2", KT - 1)
            first_tile(C_UP, RMS_BASE["norm2"])
            pe.wait_ge(w_lo, C_UP + 2)
            products(bank(1), chunk_blocks(1, normed), True, True).then_inc(w_used, 1)
            tiles(C_UP + 2, N_UP + 2, 2 * FF_T - 2)
            with pe.Fori(0, KT // 2) as i:
                for b in range(2):
                    pe.wait_ge(evac[b], i + N_DOWN // 2)
                    for j in range(DOWN_C):
                        pe.wait_ge(ff_lo, min(KT * (j + 1), FF_T) + 1)
                        s = (DOWN_C * b + j) % 2
                        pe.wait_ge(w_lo, i * (2 * DOWN_C) + (C_DOWN + DOWN_C * b + j + 1))
                        n = min(KT, FF_T - KT * j)
                        products(bank(b), chunk_blocks(s, lambda k: (FHI[:, KT * j + k, :], FLO[:, KT * j + k, :]), n),
                                 j == 0, j == DOWN_C - 1).then_inc(w_used, 1)
            pe.drain().then_inc(layer_end, 1)

    ctx.close()


def _blocks(w, n_blocks):
    layers, rows, cols = w.shape
    k = rows // P
    chunks = -(-k // n_blocks)
    b = w.reshape(layers, k, P, cols // P, P).transpose(0, 3, 2, 1, 4)
    if chunks * n_blocks != k:
        b = np.concatenate([b, np.zeros(b.shape[:3] + (chunks * n_blocks - k, P), b.dtype)], axis=3)
    b = b.reshape(layers, cols // P, P, chunks, n_blocks * P).transpose(0, 1, 3, 2, 4)
    return np.ascontiguousarray(b.reshape(layers, cols // P * chunks, P, n_blocks * P))


def _bias_constants():
    rel = np.arange(REL) - (SEQ - 1)
    n = np.abs(rel)
    nb = BUCKETS // 2
    exact = nb // 2
    large = exact + (np.log(np.maximum(n, 1).astype(np.float32) / exact) / math.log(MAX_DISTANCE / exact)
                     * (nb - exact)).astype(np.int32)
    bucket = np.where(rel > 0, nb, 0) + np.where(n < exact, n, np.minimum(large, nb - 1))
    onehot = (np.arange(BUCKETS)[:, None] == bucket[None, :]).astype(np.float32)
    count = sum(((n % d == 0) & (n // d <= w // 2 // d)).astype(np.int32) for w, d in PATTERNS)
    log_count = np.where(count > 0, np.log(np.maximum(count, 1)), NEG).astype(np.float32)
    return onehot, np.ascontiguousarray(np.broadcast_to(log_count, (HEADS, REL)))


def _constants():
    i, j = np.arange(P)[:, None], np.arange(P)[None, :]
    made = {"ident": i == j, "ones": i >= 0 * j, "le": i <= j, "ge": i >= j, "gt": i > j, "lt": i < j,
            "headones": i // HEAD_DIM == j // HEAD_DIM}
    return np.ascontiguousarray(np.stack([made[n] for n in CONSTS], axis=1).astype(np.float32))


def kernel(x, rel_table, norm1_g, w_in, q_norm_g, k_norm_g, ssd_conv_w, ssd_conv_b, ssd_dt_bias, ssd_a_log, ssd_d,
           ssd_norm_g, sc_conv_w, sc_conv_b, w_out, norm2_g, ffn_w_up, ffn_conv_w, ffn_conv_b, ffn_w_down):
    import concourse.bacc as bacc
    from concourse.bass_utils import run_bass_kernel_spmd

    f = np.asarray
    w = f(w_in)
    ends = np.cumsum([512, 512, 512, 1024, 1536, 32, 512, 512, 512])
    wq, wk, wv, wz, wx, wdt, wb, wc, wxin = np.split(w, ends[:-1], axis=2)
    v_chunks = wv.reshape(DEPTH, 4, 2, P, 512).transpose(0, 1, 3, 2, 4).reshape(DEPTH, 4, P, CHUNK)
    sc = np.stack([_blocks(m, KT) for m in (wc, wxin, wb)], axis=2).reshape(DEPTH, 12, P, CHUNK)
    win = np.concatenate([_blocks(wx, KT), _blocks(wq, KT), _blocks(wk, KT), v_chunks, _blocks(wz, KT), sc], axis=1)

    def padded(m):
        m = m.reshape(m.shape[:-1] + (2, SSD_HEADS))
        m = np.concatenate([m, np.zeros(m.shape[:-1] + (DIR - SSD_HEADS,), m.dtype)], axis=-1)
        return m.reshape(m.shape[:-2] + (2 * DIR,))

    wd = padded(wdt).reshape(DEPTH, 2, 4, P, 64).transpose(0, 1, 3, 2, 4).reshape(DEPTH * 2, P, 256)
    up = np.stack(np.split(_blocks(f(ffn_w_up), KT), 2, axis=1), axis=2)

    def columns(m):
        return m.reshape(DEPTH, m.shape[1], -1, P).transpose(0, 3, 2, 1)

    def rows(m):
        return np.broadcast_to(m[:, None, :], (DEPTH, P, m.shape[-1]))

    conv7 = columns(np.concatenate([f(ssd_conv_w), f(ssd_conv_b)[:, None]], axis=1))
    conv_sc = columns(np.concatenate([f(sc_conv_w), f(sc_conv_b)[:, None]], axis=1))
    conv_ff = columns(np.concatenate([f(ffn_conv_w), f(ffn_conv_b)[:, None]], axis=1))
    conv_ff = np.stack(np.split(conv_ff, 2, axis=2), axis=3)
    params = np.concatenate([p.reshape(DEPTH, P, -1) for p in (
        columns(f(norm1_g)[:, None]), columns(f(norm2_g)[:, None]),
        np.concatenate([f(q_norm_g)] * 2, axis=1)[:, :, None], np.concatenate([f(k_norm_g)] * 2, axis=1)[:, :, None],
        conv7, columns(np.repeat(f(ssd_d), SSD_W // SSD_HEADS, axis=1)[:, None]), columns(f(ssd_norm_g)[:, None]),
        conv_sc, conv_ff,
        rows(padded(f(ssd_dt_bias).reshape(DEPTH, 32))), rows(padded(f(ssd_a_log).reshape(DEPTH, 32))),
    )], axis=2)
    assert params.shape[2] == PA_N
    w_o = np.concatenate([f(w_out)[:, :512], f(w_out)[:, 1536:], f(w_out)[:, 512:1536]], axis=1)
    w_o = _blocks(w_o, KT)[:, [2 * m + j for m, j in OUT_ORDER]]
    onehot, log_count = _bias_constants()
    arrays = {
        "constants": _constants(), "x_t": f(x)[0].T, "onehot": onehot, "log_count": log_count,
        "rel_table": f(rel_table), "params": params,
        "w_in": win.reshape(-1, P, CHUNK), "w_dt": wd,
        "w_out": w_o.reshape(-1, P, CHUNK),
        "w_up": up.reshape(-1, P, CHUNK),
        "w_down": _blocks(f(ffn_w_down), KT).reshape(-1, P, CHUNK),
    }
    arrays = {n: np.ascontiguousarray(m) for n, m in arrays.items()}
    nc = bacc.Bacc("TRN2", target_bir_lowering=False, num_devices=1)
    aps = {n: nc.dram_tensor(n, m.shape, mybir.dt.from_np(m.dtype), kind="ExternalInput").ap() for n, m in arrays.items()}
    aps["out_t"] = nc.dram_tensor("out_t", (D_MODEL, SEQ), F32, kind="ExternalOutput").ap()
    build_trunk(nc, aps)
    r = run_bass_kernel_spmd(nc, [arrays], core_ids=[0])
    return np.ascontiguousarray(r.results[0]["out_t"].T)[None]
```
